# Optimizing a Trainium2 kernel written in Bass

```python
import math
import jax
import jax.numpy as jnp
from jax import lax
import numpy as np
import jax, jax.numpy as jnp

D_MODEL = 1024
BATCH = 1
SEQ = 256
DEPTH = 1

D_MIX = D_MODEL
D_NSA = D_MIX // 2
D_CONV = D_MIX - D_NSA
HEAD_DIM = 64
N_HEADS = D_NSA // HEAD_DIM
N_KV = 2
REP = N_HEADS // N_KV
KV_W = N_KV * HEAD_DIM
N_GATES = 3 * N_HEADS
D_IN = D_NSA + 6 * KV_W + N_GATES + 3 * D_CONV
L_CMP = 32
S_CMP = 16
L_SLC = 64
N_SEL = 16
WINDOW = 512
Q_BLOCK = 128
CMP_HIDDEN = 256
CONV_W = 3
D_FF = 2816
N_BUCKETS = 32
MAX_DIST = 128
RMS_EPS = 1e-6
NEG = -1e30
FORCE_BONUS = 1e4


def rms_norm(x, g):
    xf = x.astype(jnp.float32)
    y = xf * lax.rsqrt(jnp.mean(xf * xf, axis=-1, keepdims=True) + RMS_EPS)
    return (y * g.astype(jnp.float32)).astype(x.dtype)

def causal_dwconv(x, w):
    return lax.conv_general_dilated(
        x, w[:, None, :].astype(x.dtype), window_strides=(1,),
        padding=[(CONV_W - 1, 0)], dimension_numbers=('NWC', 'WIO', 'NWC'),
        feature_group_count=x.shape[-1])

def t5_bucket(dist):
    max_exact = N_BUCKETS // 2
    d = jnp.maximum(dist, 0)
    df = jnp.maximum(d, 1).astype(jnp.float32)
    large = max_exact + (jnp.log(df / max_exact) / math.log(MAX_DIST / max_exact)
                         * (N_BUCKETS - max_exact)).astype(jnp.int32)
    return jnp.where(d < max_exact, d, jnp.minimum(large, N_BUCKETS - 1))

def masked_softmax(logits, mask):
    z = jnp.where(mask, logits.astype(jnp.float32), NEG)
    p = jax.nn.softmax(z, axis=-1)
    return p * jnp.any(mask, axis=-1, keepdims=True)

def compress_kv(kv, pe, w1, w2):
    B, S, G, dh = kv.shape
    n_cmp = (S - L_CMP) // S_CMP + 1
    idx = jnp.arange(n_cmp)[:, None] * S_CMP + jnp.arange(L_CMP)[None, :]
    blk = kv[:, idx] + pe[None, None, :, None, :]
    blk = blk.transpose(0, 3, 1, 2, 4).reshape(B, G, n_cmp, L_CMP * dh)
    return jax.nn.gelu(blk @ w1, approximate=True) @ w2

def nsa_attention(q, k_c, v_c, k_s, v_s, k_w, v_w, gate_logits,
                  pe_k, pe_v, wk1, wk2, wv1, wv2, rel_bias):
    B, S = q.shape[0], q.shape[1]
    n_cmp = (S - L_CMP) // S_CMP + 1
    n_slc = S // L_SLC
    n_sel = min(N_SEL, n_slc)
    nqb = S // Q_BLOCK
    scale = HEAD_DIM ** -0.5
    t = jnp.arange(S)
    tab = rel_bias.reshape(N_KV, REP, N_BUCKETS)
    qg = q.reshape(B, S, N_KV, REP, HEAD_DIM).transpose(0, 2, 3, 1, 4)

    kc = compress_kv(k_c, pe_k, wk1, wk2)
    vc = compress_kv(v_c, pe_v, wv1, wv2)
    c_start = jnp.arange(n_cmp) * S_CMP
    dist_c = t[:, None] - (c_start + L_CMP - 1)[None, :]
    logits_c = (jnp.einsum('bgrsd,bgnd->bgrsn', qg, kc) * scale
                + tab[:, :, t5_bucket(dist_c)])
    p_c = masked_softmax(logits_c, dist_c >= 0)
    o_c = jnp.einsum('bgrsn,bgnd->bgrsd', p_c.astype(vc.dtype), vc)

    s_start = jnp.arange(n_slc) * L_SLC
    overlap = jnp.clip(jnp.minimum(c_start[:, None] + L_CMP, s_start[None, :] + L_SLC)
                       - jnp.maximum(c_start[:, None], s_start[None, :]), 0, None)
    overlap = overlap.astype(jnp.float32) / L_CMP
    imp = jnp.einsum('bgrsn,nj->bgsj', p_c, overlap)
    j = jnp.arange(n_slc)[None, :]
    cur = (t // L_SLC)[:, None]
    forced = (j == 0) | (j == cur) | (j == cur - 1)
    score = jnp.where(j <= cur, imp + jnp.where(forced, FORCE_BONUS, 0.0), NEG)
    top_val, top_idx = lax.top_k(score, n_sel)
    top_ok = top_val > 0.5 * NEG

    k_sb = k_s.reshape(B, n_slc, L_SLC, N_KV, HEAD_DIM).transpose(0, 3, 1, 2, 4)
    v_sb = v_s.reshape(B, n_slc, L_SLC, N_KV, HEAD_DIM).transpose(0, 3, 1, 2, 4)
    k_wp = jnp.pad(k_w, ((0, 0), (WINDOW, 0), (0, 0), (0, 0)))
    v_wp = jnp.pad(v_w, ((0, 0), (WINDOW, 0), (0, 0), (0, 0)))
    bi = jnp.arange(B)[:, None, None, None]
    gi = jnp.arange(N_KV)[None, :, None, None]

    def block_fn(args):
        n, q_b, idx_b, ok_b = args
        t_b = n * Q_BLOCK + jnp.arange(Q_BLOCK)
        ks = k_sb[bi, gi, idx_b].reshape(B, N_KV, Q_BLOCK, n_sel * L_SLC, HEAD_DIM)
        vs = v_sb[bi, gi, idx_b].reshape(B, N_KV, Q_BLOCK, n_sel * L_SLC, HEAD_DIM)
        pos = (idx_b[..., None] * L_SLC + jnp.arange(L_SLC)).reshape(
            B, N_KV, Q_BLOCK, n_sel * L_SLC)
        dist_s = t_b[None, None, :, None] - pos
        m_s = (dist_s >= 0) & jnp.repeat(ok_b, L_SLC, axis=-1)
        bias_s = jnp.moveaxis(tab[gi, :, t5_bucket(dist_s)], -1, 2)
        logits_s = jnp.einsum('bgrqd,bgqkd->bgrqk', q_b, ks) * scale + bias_s
        p_s = masked_softmax(logits_s, m_s[:, :, None])
        o_s = jnp.einsum('bgrqk,bgqkd->bgrqd', p_s.astype(vs.dtype), vs)
        kw = lax.dynamic_slice_in_dim(k_wp, n * Q_BLOCK, Q_BLOCK + WINDOW, axis=1)
        vw = lax.dynamic_slice_in_dim(v_wp, n * Q_BLOCK, Q_BLOCK + WINDOW, axis=1)
        s_w = n * Q_BLOCK - WINDOW + jnp.arange(Q_BLOCK + WINDOW)
        dist_w = t_b[:, None] - s_w[None, :]
        m_w = (dist_w >= 0) & (dist_w < WINDOW) & (s_w[None, :] >= 0)
        logits_w = (jnp.einsum('bgrqd,bkgd->bgrqk', q_b, kw) * scale
                    + tab[:, :, t5_bucket(dist_w)])
        p_w = masked_softmax(logits_w, m_w)
        o_w = jnp.einsum('bgrqk,bkgd->bgrqd', p_w.astype(vw.dtype), vw)
        return o_s, o_w

    q_blocks = jnp.moveaxis(qg.reshape(B, N_KV, REP, nqb, Q_BLOCK, HEAD_DIM), 3, 0)
    idx_blocks = jnp.moveaxis(top_idx.reshape(B, N_KV, nqb, Q_BLOCK, n_sel), 2, 0)
    ok_blocks = jnp.moveaxis(top_ok.reshape(B, N_KV, nqb, Q_BLOCK, n_sel), 2, 0)
    o_s, o_w = lax.map(block_fn, (jnp.arange(nqb), q_blocks, idx_blocks, ok_blocks))
    o_s = jnp.moveaxis(o_s, 0, 3).reshape(B, N_KV, REP, S, HEAD_DIM)
    o_w = jnp.moveaxis(o_w, 0, 3).reshape(B, N_KV, REP, S, HEAD_DIM)

    g = jax.nn.sigmoid(gate_logits.astype(jnp.float32)).reshape(B, S, N_KV, REP, 3)
    g = g.transpose(0, 2, 3, 1, 4).astype(q.dtype)
    o = g[..., 0:1] * o_c + g[..., 1:2] * o_s + g[..., 2:3] * o_w
    return o.transpose(0, 3, 1, 2, 4).reshape(B, S, D_NSA)

def short_conv_mixer(b_gate, c_gate, x_t, conv_w):
    return b_gate * causal_dwconv(c_gate * x_t, conv_w)

def split_points():
    sizes = [D_NSA] + [KV_W] * 6 + [N_GATES, D_CONV, D_CONV]
    pts, acc = [], 0
    for s in sizes:
        acc += s
        pts.append(acc)
    return pts

def first_inputs(seed: int = 0) -> dict:
    key = jax.random.key(seed)
    ks = jax.random.split(key, 20)

    def nrm(k, shape, scale):
        return jax.random.normal(k, shape, jnp.float32) * scale

    return {
        'x': nrm(ks[0], (BATCH, SEQ, D_MODEL), 1.0),
        'norm_mix_pre': 1.0 + nrm(ks[1], (DEPTH, D_MODEL), 0.05),
        'norm_mix_post': 1.0 + nrm(ks[2], (DEPTH, D_MODEL), 0.05),
        'norm_ffn_pre': 1.0 + nrm(ks[3], (DEPTH, D_MODEL), 0.05),
        'norm_ffn_post': 1.0 + nrm(ks[4], (DEPTH, D_MODEL), 0.05),
        'w_in': nrm(ks[5], (DEPTH, D_MODEL, D_IN), D_MODEL ** -0.5),
        'pe_cmp_k': nrm(ks[6], (DEPTH, L_CMP, HEAD_DIM), 0.5),
        'pe_cmp_v': nrm(ks[7], (DEPTH, L_CMP, HEAD_DIM), 0.5),
        'w_cmp_k1': nrm(ks[8], (DEPTH, L_CMP * HEAD_DIM, CMP_HIDDEN), (L_CMP * HEAD_DIM) ** -0.5),
        'w_cmp_k2': nrm(ks[9], (DEPTH, CMP_HIDDEN, HEAD_DIM), CMP_HIDDEN ** -0.5),
        'w_cmp_v1': nrm(ks[10], (DEPTH, L_CMP * HEAD_DIM, CMP_HIDDEN), (L_CMP * HEAD_DIM) ** -0.5),
        'w_cmp_v2': nrm(ks[11], (DEPTH, CMP_HIDDEN, HEAD_DIM), CMP_HIDDEN ** -0.5),
        'rel_bias': nrm(ks[12], (N_HEADS, N_BUCKETS), 0.5),
        'conv_mix_w': nrm(ks[13], (DEPTH, CONV_W, D_CONV), CONV_W ** -0.5),
        'w_out': nrm(ks[14], (DEPTH, D_MIX, D_MODEL), D_MIX ** -0.5),
        'w_ffn_up': nrm(ks[15], (DEPTH, D_MODEL, 2 * D_FF), D_MODEL ** -0.5),
        'ffn_conv_w': nrm(ks[16], (DEPTH, CONV_W, 2 * D_FF), CONV_W ** -0.5),
        'w_ffn_down': nrm(ks[17], (DEPTH, D_FF, D_MODEL), D_FF ** -0.5),
    }

def first_block(x, norm_mix_pre, norm_mix_post, norm_ffn_pre, norm_ffn_post, w_in,
              pe_cmp_k, pe_cmp_v, w_cmp_k1, w_cmp_k2, w_cmp_v1, w_cmp_v2, rel_bias,
              conv_mix_w, w_out, w_ffn_up, ffn_conv_w, w_ffn_down):
    B, S, _ = x.shape
    for l in range(DEPTH):
        h = rms_norm(x, norm_mix_pre[l])
        u = h @ w_in[l]
        q, k_c, v_c, k_s, v_s, k_w, v_w, gl, b_g, c_g, x_t = jnp.split(
            u, split_points(), axis=-1)
        kv = lambda a: a.reshape(B, S, N_KV, HEAD_DIM)
        o_nsa = nsa_attention(q.reshape(B, S, N_HEADS, HEAD_DIM),
                              kv(k_c), kv(v_c), kv(k_s), kv(v_s), kv(k_w), kv(v_w), gl,
                              pe_cmp_k[l], pe_cmp_v[l], w_cmp_k1[l], w_cmp_k2[l],
                              w_cmp_v1[l], w_cmp_v2[l], rel_bias)
        o_conv = short_conv_mixer(b_g, c_g, x_t, conv_mix_w[l])
        y = jnp.concatenate([o_nsa, o_conv], axis=-1) @ w_out[l]
        x = x + rms_norm(y, norm_mix_post[l])
        h = rms_norm(x, norm_ffn_pre[l])
        gu = causal_dwconv(h @ w_ffn_up[l], ffn_conv_w[l])
        g, up = jnp.split(gu, 2, axis=-1)
        y = (jax.nn.gelu(g, approximate=True) * up) @ w_ffn_down[l]
        x = x + rms_norm(y, norm_ffn_post[l])
    return x


N_META = 16
CONV_CH = 512
CONV_KERNEL = 31
RWKV_WIDTH = 512
RWKV_HEAD = 64
RWKV_HEADS = RWKV_WIDTH // RWKV_HEAD
RANK_W = 64
RANK_A = 64
RANK_G = 128
N_BRANCH = 2
SHIFT_TOTAL = 3 * RWKV_WIDTH + RANK_W + RANK_A + RANK_G
IN_SPLITS = [CONV_CH, 2 * CONV_CH, 2 * CONV_CH + SHIFT_TOTAL]
IN_TOTAL = 2 * CONV_CH + SHIFT_TOTAL + N_BRANCH * D_MODEL
RWKV_SPLITS = [RWKV_WIDTH, 2 * RWKV_WIDTH, 3 * RWKV_WIDTH, 3 * RWKV_WIDTH + RANK_W, 3 * RWKV_WIDTH + RANK_W + RANK_A]
PEER_HEADS = 8
PEER_NKEYS = 128
PEER_EXPERTS = PEER_NKEYS * PEER_NKEYS
PEER_DHALF = 128
PEER_TOPK = 16
TOK_BLOCK = 256
LN_EPS = 1e-5
GN_EPS = 64e-5


def rmsnorm(x, g):
    xf = x.astype(jnp.float32)
    y = xf * lax.rsqrt(jnp.mean(xf * xf, axis=-1, keepdims=True) + RMS_EPS)
    return (y * g.astype(jnp.float32)).astype(x.dtype)

def token_shift(z):
    return jnp.pad(z[:, :-1], ((0, 0), (1, 0), (0, 0)))

def conformer_conv(val, gate, conv_w, conv_b, ln_g, ln_b, w_out):
    u = val * jax.nn.sigmoid(gate)
    y = lax.conv_general_dilated(
        u, conv_w[:, None, :].astype(u.dtype), window_strides=(1,),
        padding=[(CONV_KERNEL - 1, 0)], dimension_numbers=('NWC', 'WIO', 'NWC'),
        feature_group_count=CONV_CH) + conv_b
    yf = y.astype(jnp.float32)
    mean = jnp.mean(yf, axis=-1, keepdims=True)
    var = jnp.mean(jnp.square(yf - mean), axis=-1, keepdims=True)
    yn = (yf - mean) * lax.rsqrt(var + LN_EPS) * ln_g + ln_b
    return jax.nn.silu(yn).astype(val.dtype) @ w_out

def wkv7_scan(r, decay, k, v, kk, a):
    def step(S, inp):
        r_t, w_t, k_t, v_t, kk_t, a_t = inp
        sa = jnp.einsum('bhvk,bhk->bhv', S, kk_t)
        S = (S * w_t[:, :, None, :]
             - sa[..., None] * (kk_t * a_t)[:, :, None, :]
             + v_t[..., None] * k_t[:, :, None, :])
        return S, jnp.einsum('bhvk,bhk->bhv', S, r_t)
    B, T, H, N = r.shape
    S0 = jnp.zeros((B, H, N, N), jnp.float32)
    xs = tuple(jnp.moveaxis(z, 1, 0) for z in (r, decay, k, v, kk, a))
    _, o = lax.scan(step, S0, xs)
    return jnp.moveaxis(o, 0, 1)

def rwkv7_mix(z, mu, w0, w_up, a0, a_up, g_up, k_k, k_a, r_k, gn_g, gn_b, w_out):
    B, T, _ = z.shape
    zf = z.astype(jnp.float32)
    zf = zf + (token_shift(zf) - zf) * mu
    r, k, v, lw, la, lg = jnp.split(zf, RWKV_SPLITS, axis=-1)
    w = -jax.nn.softplus(-(w0 + jnp.tanh(lw) @ w_up)) - 0.5
    decay = jnp.exp(-jnp.exp(w))
    a = jax.nn.sigmoid(a0 + la @ a_up)
    g = jax.nn.sigmoid(lg) @ g_up
    hd = lambda t: t.reshape(B, T, RWKV_HEADS, RWKV_HEAD)
    kk = hd(k * k_k)
    kk = kk * lax.rsqrt(jnp.maximum(jnp.sum(kk * kk, axis=-1, keepdims=True), 1e-24))
    k = k * (1.0 + (a - 1.0) * k_a)
    r_h, k_h, v_h, a_h = hd(r), hd(k), hd(v), hd(a)
    o = wkv7_scan(r_h, hd(decay), k_h, v_h, kk, a_h)
    mean = jnp.mean(o, axis=-1, keepdims=True)
    var = jnp.mean(jnp.square(o - mean), axis=-1, keepdims=True)
    o = ((o - mean) * lax.rsqrt(var + GN_EPS)).reshape(B, T, RWKV_WIDTH) * gn_g + gn_b
    bonus = jnp.sum(r_h * k_h * r_k, axis=-1, keepdims=True) * v_h
    o = (o + bonus.reshape(B, T, RWKV_WIDTH)) * g
    return o.astype(z.dtype) @ w_out

def peer_ffn(x, w_q, sub_keys, expert_u, expert_v):
    B, T, D = x.shape
    n_tok = B * T
    n_blocks = -(-n_tok // TOK_BLOCK)
    pad = n_blocks * TOK_BLOCK - n_tok
    xt = jnp.pad(x.reshape(n_tok, D), ((0, pad), (0, 0))).reshape(n_blocks, TOK_BLOCK, D)
    K = PEER_TOPK

    def block(xb):
        q = (xb @ w_q).reshape(TOK_BLOCK, PEER_HEADS, 2, PEER_DHALF)
        s = jnp.einsum('thcd,hcnd->thcn', q, sub_keys).astype(jnp.float32)
        top_s, top_i = lax.top_k(s, K)
        cand = top_s[:, :, 0, :, None] + top_s[:, :, 1, None, :]
        best_s, best_c = lax.top_k(cand.reshape(TOK_BLOCK, PEER_HEADS, K * K), K)
        i1 = jnp.take_along_axis(top_i[:, :, 0], best_c // K, axis=-1)
        i2 = jnp.take_along_axis(top_i[:, :, 1], best_c % K, axis=-1)
        e = (i1 * PEER_NKEYS + i2).reshape(TOK_BLOCK, PEER_HEADS * K)
        gate = jax.nn.softmax(best_s, axis=-1).reshape(TOK_BLOCK, PEER_HEADS * K)
        u = expert_u[e]
        act = jax.nn.gelu(jnp.einsum('td,ted->te', xb, u), approximate=False)
        coef = (gate * act.astype(jnp.float32)).astype(xb.dtype)
        return jnp.einsum('te,ted->td', coef, expert_v[e])

    y = lax.map(block, xt)
    return y.reshape(n_blocks * TOK_BLOCK, D)[:n_tok].reshape(B, T, D)

def second_inputs(seed: int = 0) -> dict:
    key = jax.random.key(seed)
    ks = jax.random.split(key, 32)
    f32 = jnp.float32
    L = DEPTH
    D = D_MODEL

    def nrm(k, shape, s):
        return jax.random.normal(k, shape, f32) * s

    return {
        "x": nrm(ks[0], (BATCH, SEQ, D), 1.0),
        "meta_tokens": nrm(ks[1], (N_META, D), 1.0),
        "g_mix": 1.0 + nrm(ks[2], (L, D), 0.01),
        "w_in": nrm(ks[3], (L, D, IN_TOTAL), D ** -0.5),
        "conv_w": nrm(ks[4], (L, CONV_KERNEL, CONV_CH), CONV_KERNEL ** -0.5),
        "conv_b": nrm(ks[5], (L, CONV_CH), 0.01),
        "conv_ln_g": 1.0 + nrm(ks[6], (L, CONV_CH), 0.01),
        "conv_ln_b": nrm(ks[7], (L, CONV_CH), 0.01),
        "w_conv_out": nrm(ks[8], (L, CONV_CH, D), CONV_CH ** -0.5),
        "mu_shift": jax.random.uniform(ks[9], (L, SHIFT_TOTAL), f32),
        "w0": jax.random.uniform(ks[10], (L, RWKV_WIDTH), f32, -6.0, -1.0),
        "w_up": nrm(ks[11], (L, RANK_W, RWKV_WIDTH), 0.1 * RANK_W ** -0.5),
        "a0": nrm(ks[12], (L, RWKV_WIDTH), 0.1),
        "a_up": nrm(ks[13], (L, RANK_A, RWKV_WIDTH), 0.1 * RANK_A ** -0.5),
        "g_up": nrm(ks[14], (L, RANK_G, RWKV_WIDTH), RANK_G ** -0.5),
        "k_k": 0.85 + nrm(ks[15], (L, RWKV_WIDTH), 0.02),
        "k_a": 1.0 + nrm(ks[16], (L, RWKV_WIDTH), 0.02),
        "r_k": nrm(ks[17], (L, RWKV_HEADS, RWKV_HEAD), 0.1),
        "gn_g": 1.0 + nrm(ks[18], (L, RWKV_WIDTH), 0.01),
        "gn_b": nrm(ks[19], (L, RWKV_WIDTH), 0.01),
        "w_rwkv_out": nrm(ks[20], (L, RWKV_WIDTH, D), RWKV_WIDTH ** -0.5),
        "w_o": nrm(ks[21], (L, D, D), D ** -0.5),
        "g_ffn": 1.0 + nrm(ks[22], (L, D), 0.01),
        "w_q": nrm(ks[23], (L, D, PEER_HEADS * 2 * PEER_DHALF), D ** -0.5),
        "sub_keys": nrm(ks[24], (L, PEER_HEADS, 2, PEER_NKEYS, PEER_DHALF), PEER_DHALF ** -0.5),
        "expert_u": nrm(ks[25], (L, PEER_EXPERTS, D), D ** -0.5),
        "expert_v": nrm(ks[26], (L, PEER_EXPERTS, D), PEER_HEADS ** -0.5),
        "g_final": 1.0 + nrm(ks[27], (D,), 0.01),
    }

def second_block(x, meta_tokens, g_mix, w_in, conv_w, conv_b, conv_ln_g, conv_ln_b, w_conv_out,
              mu_shift, w0, w_up, a0, a_up, g_up, k_k, k_a, r_k, gn_g, gn_b, w_rwkv_out,
              w_o, g_ffn, w_q, sub_keys, expert_u, expert_v, g_final):
    B = x.shape[0]
    meta = jnp.broadcast_to(meta_tokens[None].astype(x.dtype), (B, N_META, D_MODEL))
    h = jnp.concatenate([meta, x], axis=1)
    for l in range(DEPTH):
        z = rmsnorm(h, g_mix[l]) @ w_in[l]
        conv_val, conv_gate, rwkv_in, gate_logits = jnp.split(z, IN_SPLITS, axis=-1)
        y_a = conformer_conv(conv_val, conv_gate, conv_w[l], conv_b[l], conv_ln_g[l], conv_ln_b[l], w_conv_out[l])
        y_b = rwkv7_mix(rwkv_in, mu_shift[l], w0[l], w_up[l], a0[l], a_up[l], g_up[l],
                        k_k[l], k_a[l], r_k[l], gn_g[l], gn_b[l], w_rwkv_out[l])
        gate_a, gate_b = jnp.split(jax.nn.sigmoid(gate_logits), N_BRANCH, axis=-1)
        h = h + (gate_a * y_a + gate_b * y_b) @ w_o[l]
        h = h + peer_ffn(rmsnorm(h, g_ffn[l]), w_q[l], sub_keys[l], expert_u[l], expert_v[l])
    return rmsnorm(h, g_final)[:, N_META:]


def setup_inputs(seed=0):
    out = dict(first_inputs(seed))
    for name, value in second_inputs(seed + 1).items():
        if name != "x":
            out[name + "_2"] = value
    return out


def reference(
    x, norm_mix_pre, norm_mix_post, norm_ffn_pre, norm_ffn_post, w_in, pe_cmp_k, pe_cmp_v,
    w_cmp_k1, w_cmp_k2, w_cmp_v1, w_cmp_v2, rel_bias, conv_mix_w, w_out, w_ffn_up, ffn_conv_w,
    w_ffn_down, meta_tokens_2, g_mix_2, w_in_2, conv_w_2, conv_b_2, conv_ln_g_2, conv_ln_b_2,
    w_conv_out_2, mu_shift_2, w0_2, w_up_2, a0_2, a_up_2, g_up_2, k_k_2, k_a_2, r_k_2, gn_g_2,
    gn_b_2, w_rwkv_out_2, w_o_2, g_ffn_2, w_q_2, sub_keys_2, expert_u_2, expert_v_2, g_final_2,
):
    x = first_block(
        x, norm_mix_pre, norm_mix_post, norm_ffn_pre, norm_ffn_post, w_in, pe_cmp_k, pe_cmp_v,
        w_cmp_k1, w_cmp_k2, w_cmp_v1, w_cmp_v2, rel_bias, conv_mix_w, w_out, w_ffn_up,
        ffn_conv_w, w_ffn_down,
    )
    return second_block(
        x, meta_tokens_2, g_mix_2, w_in_2, conv_w_2, conv_b_2, conv_ln_g_2, conv_ln_b_2,
        w_conv_out_2, mu_shift_2, w0_2, w_up_2, a0_2, a_up_2, g_up_2, k_k_2, k_a_2, r_k_2,
        gn_g_2, gn_b_2, w_rwkv_out_2, w_o_2, g_ffn_2, w_q_2, sub_keys_2, expert_u_2, expert_v_2,
        g_final_2,
    )


_drawn_inputs = setup_inputs


def setup_inputs(seed=0):
    import zlib

    import numpy as np

    out = dict(_drawn_inputs(seed))
    spreads = {}
    factors = {'g_mix_2': 6.993,
     'conv_b_2': 64.0,
     'conv_ln_g_2': 64.0,
     'conv_ln_b_2': 64.0,
     'w_up_2': 64.0,
     'a0_2': 4.683,
     'a_up_2': 4.959,
     'k_k_2': 64.0,
     'k_a_2': 7.468,
     'gn_g_2': 64.0,
     'gn_b_2': 64.0,
     'g_ffn_2': 42.656,
     'g_final_2': 31.536,
     'conv_w_2': 3.877,
     'w_conv_out_2': 3.268,
     'w0_2': 6.573,
     'w_q_2': 5.719,
     'sub_keys_2': 5.628,
     'expert_u_2': 6.911,
     'expert_v_2': 5.537}
    for name, (base, spread) in spreads.items():
        noise = np.random.default_rng([zlib.crc32(name.encode()), seed]).standard_normal(out[name].shape)
        drawn = base * np.exp(spread * noise) if base else spread * noise
        out[name] = jnp.asarray(drawn.astype(out[name].dtype))
    for name, factor in factors.items():
        out[name] = (out[name] * factor).astype(out[name].dtype)
    return out
```

```python
import numpy as np
import concourse.bass as bass
import concourse.mybir as mybir
from contextlib import ExitStack

P = 128
D = 1024
KD = D // P
TX = 256
N_META = 16
T2 = TX + N_META
TW = KD * P
RING = 6

HD = 64
N_HEADS = 8
N_KV = 2
REP = N_HEADS // N_KV
N_CMP = (TX - 32) // 16 + 1
D_FF = 2816
NF = D_FF // P
NEG = -1e30
EPS = 1e-6
SCALE = HD ** -0.5
Z1 = 24
ZQ, ZKC, ZVC, ZKS, ZVS, ZKW, ZVW, ZB, ZC, ZX = 0, 4, 6, 8, 9, 10, 11, 12, 16, 20

Z2 = 38
NCH = T2 // 16
CH = 16
LN_EPS = 1e-5
GN_EPS = 64e-5
TAPS = 31
NE = 128
TOPK = 16

F32 = mybir.dt.float32
U32 = mybir.dt.uint32
ALU = mybir.AluOpType
ACT = mybir.ActivationFunctionType
AX = mybir.AxisListType.X


def column_layout():
    at, n = {}, 0
    for name, width in [
        ("mix_pre", 8), ("mix_post", 8), ("ffn_pre", 8), ("ffn_post", 8), ("mix2", 8), ("ffn2", 8),
        ("final", 8), ("conv_mix", 12), ("ffn_conv", 3 * 2 * NF), ("pe", 32), ("gates", KD * 24),
        ("w2k", 256), ("w2v", 128), ("conv_w", 4 * TAPS), ("conv_b", 4), ("ln_g", 4), ("ln_b", 4),
        ("mu", 14), ("w0", 4), ("a0", 4), ("k_k", 4), ("k_a", 4), ("r_k", 4), ("gn_g", 4), ("gn_b", 4),
        ("wa_up", 512), ("g_up", 512),
    ]:
        at[name] = (n, width)
        n += width
    return at, n


COLS, N_COLS = column_layout()


def constant_layout():
    at, n = {}, 0
    for name, width in [("ident", P), ("ones", P), ("flip", P), ("headones", P), ("identhead", HD), ("lower", P), ("upper", P), ("upper_in", P),
                        ("chunk", 8), ("rowmask", 2), ("onehot", 512), ("iota", P), ("scanmask", 4 * T2)]:
        at[name] = (n, width)
        n += width
    return at, n


CONSTS, N_CONSTS = constant_layout()


def shape_constants():
    c = np.zeros((P, N_CONSTS), np.float32)

    def put(name, value):
        o, w = CONSTS[name]
        c[:value.shape[0], o:o + w] = value

    i = np.arange(P)
    same = i[:, None] // CH == i[None, :] // CH
    put("ident", np.eye(P))
    put("ones", np.ones((P, P)))
    put("flip", np.eye(P)[::-1])
    put("headones", (i[:, None] // HD == i[None, :] // HD) * 1.0)
    put("identhead", (i[:, None] % HD == np.arange(HD)[None, :]) * 1.0)
    put("lower", (same & (i[:, None] > i[None, :])) * 1.0)
    put("upper", (same & (i[:, None] < i[None, :])) * 1.0)
    put("upper_in", (same & (i[:, None] <= i[None, :])) * 1.0)
    put("chunk", (i[:, None] // CH == np.arange(8)[None, :]) * 1.0)
    put("rowmask", np.stack([i >= 31, i >= 0], 1) * 1.0)
    dist = 255 - np.arange(512)
    far = 16 + (np.log(np.maximum(dist, 1).astype(np.float32) / np.float32(16))
                / np.float32(np.log(128 / 16)) * np.float32(16)).astype(np.int32)
    bucket = np.where(dist < 16, dist, np.minimum(far, 31))
    bucket = np.where(dist < 0, 32, bucket)
    put("onehot", (np.arange(33)[:, None] == bucket[None, :]) * 1.0)
    put("iota", np.broadcast_to(i, (P, P)) * 1.0)
    put("scanmask", np.broadcast_to((np.arange(4 * T2) % CH != 0), (P, 4 * T2)) * 1.0)
    return c


def bass_transformer_pair(nc, x_t, meta_t, cols, consts, rel, w1_in, w1_cmp, w1_out, w1_ffn,
                          w2_in, w2_mid, w2_out, w2_q, w2_sub, experts, out_t, bias_rows):
    with ExitStack() as ctx:
        def sb(name, shape, dt=F32):
            return ctx.enter_context(nc.sbuf_tensor(name, shape, dt))

        def sem(name):
            return ctx.enter_context(nc.semaphore(name))

        ring = sb("ring", [P, RING, TW])
        col = sb("col", [P, N_COLS])
        cst = sb("cst", [P, N_CONSTS])
        hx = sb("hx", [P, KD, T2])
        hn = sb("hn", [P, KD, T2])
        sq = sb("sq", [P, KD, T2])
        rms = sb("rms", [P, 2, T2])
        big = sb("big", [P, NE * TX])
        zeros = sb("zeros", [P, P])
        psum = ctx.enter_context(nc.psum_tensor("psum", [P, 8, 512], F32))

        def colv(name, a=0, b=None):
            o, w = COLS[name]
            return col[:, o + a:o + (w if b is None else b)]

        def const(name):
            o, w = CONSTS[name]
            return cst[:, o:o + w]

        def carve(at, *dims):
            n = int(np.prod(dims))
            v = big[:, at:at + n]
            if len(dims) == 2:
                v = v.rearrange("p (a b) -> p a b", a=dims[0])
            if len(dims) == 3:
                v = v.rearrange("p (a b c) -> p a b c", a=dims[0], b=dims[1])
            if len(dims) == 4:
                v = v.rearrange("p (a b c d) -> p a b c d", a=dims[0], b=dims[1], c=dims[2])
            return v

        hx1 = hx[:, :, N_META:T2]
        hn1 = hn[:, :, 0:TX]
        at = [0]

        def room(*dims):
            v = carve(at[0], *dims)
            at[0] += int(np.prod(dims))
            return v

        z1 = room(Z1, TX)
        bias_t = room(N_HEADS, 3 * P)
        cmp_in = room(2, 16, 2 * N_CMP)
        cmp_hid = room(2, 2, 2 * N_CMP)
        v_tok = room(2, 2, P)
        k_cmp = room(N_CMP)
        v_cmp = room(P)
        gates = room(2, 24)
        zbuf = room(2, REP, TX)
        zbuf_c = room(REP, N_CMP)
        red = room(2, 16)
        probs_t = room(2, 5, REP * P)
        mix_y = big[:, at[0]:at[0] + 2 * KD * TX]
        mix = room(KD, TX)
        y1 = room(KD, TX)
        bias_up = mix_y[:, 0:N_HEADS * 3 * P].rearrange("p (h k) -> p h k", h=N_HEADS)
        conv_m = room(4, TX)
        oh_tab = room(8)
        brow = room(512)
        ffn_c = room(2, 2, TX)
        ffn_g = room(2, TX)
        ffn_h = room(2, TX)
        taps = room(2, 6)
        assert at[0] <= NE * TX

        param_loaded = sem("param_loaded")
        x_loaded = sem("x_loaded")
        rel_loaded = sem("rel_loaded")
        tile_landed = [sem(f"tile_landed{s}") for s in range(RING)]
        tiles_used = sem("tiles_used")
        dve_step = sem("dve_step")
        act_step = sem("act_step")
        norm_squares = sem("norm_squares")
        norm_sums = sem("norm_sums")
        norm_mean = sem("norm_mean")
        norm_root = sem("norm_root")
        norm_out = sem("norm_out")
        in1_even = sem("in1_even")
        in1_odd = sem("in1_odd")
        gates_sum = sem("gates_sum")
        gates_ready = sem("gates_ready")
        neg_row = sem("neg_row")
        brow_sum = sem("brow_sum")
        brow_ready = sem("brow_ready")
        brow_stored = sem("brow_stored")
        bias_loaded = sem("bias_loaded")
        bias_turned = sem("bias_turned")
        bias_ready = sem("bias_ready")
        BIAS_BANKS = (0, 1, 2, 3, 6, 7)
        vtok_sum = sem("vtok_sum")
        vtok_ready = sem("vtok_ready")
        cmp_blocks = sem("cmp_blocks")
        cmp_hid_sum = sem("cmp_hid_sum")
        cmp_hid_ready = sem("cmp_hid_ready")
        cmp_sum = sem("cmp_sum")
        cmp_ready = sem("cmp_ready")
        logits_sum = sem("logits_sum")
        logits_ready = sem("logits_ready")
        exps_ready = sem("exps_ready")
        probs_ready = sem("probs_ready")
        turned = sem("turned")
        turned_copied = sem("turned_copied")
        heads_sum = sem("heads_sum")
        heads_ready = sem("heads_ready")
        conv_ready = sem("conv_ready")
        out1_ready = sem("out1_ready")
        zeros_ready = sem("zeros_ready")
        ffn_mid = sem("ffn_mid")
        ffn_scaled = sem("ffn_scaled")
        ffn_conv_g = sem("ffn_conv_g")
        ffn_conv_u = sem("ffn_conv_u")
        ffn_gelu = sem("ffn_gelu")
        ffn_hidden = sem("ffn_hidden")
        ffn_taps = sem("ffn_taps")
        ffn_copied = sem("ffn_copied")
        out_stored = sem("out_stored")
        at[0] = 0
        z2 = room(22, T2 + 1)
        alpha = room(4, T2)
        beta = room(4, T2)
        kappa = room(4, T2)
        rho = room(4, T2)
        beta_end = room(4, T2)
        kappa_end = room(4, T2)
        bonus = room(4, T2)
        gmul = room(4, T2)
        glu = room(4, T2 + TAPS - 1)
        conv_y = room(4, T2)
        chunk_decay = room(4, NCH)
        tm = room(4, 4 * P)
        scratch0 = at[0]
        gram = room(10, 4, P)
        ycol = room(4, P)
        f_t = room(4, 8, HD)
        g_c = room(4, 8, HD)
        state = room(4, 9, HD)
        top1 = at[0]
        expand = carve(scratch0, 3, 2, 8, HD)
        G_L, G_LT, G_MT, G_L2, G_L2T, G_L4, G_L4T, G_L8T, G_QT, G_RT = range(10)
        at[0] = scratch0
        delta = room(14, T2)
        at[0] = scratch0
        logdec = room(4, T2)
        cum = room(4, T2)
        a_gate = room(4, T2)
        kk = room(4, T2)
        k_new = room(4, T2)
        b_vec = room(4, T2)
        e_cum = room(4, T2)
        e_prev = room(4, T2)
        e_neg = room(4, T2)
        e_end = room(4, T2)
        assert max(at[0], top1) <= NE * TX
        sqf = sq[:, :, :].rearrange("p a b -> p (a b)")
        sq4 = sqf[:, 0:4 * T2].rearrange("p (a b) -> p a b", a=4)
        e_t = sqf[:, 0:4 * P].rearrange("p (a b) -> p a b", a=4)
        o_in = sqf[:, 4 * P:8 * P].rearrange("p (a b) -> p a b", a=4)
        o_all = sqf[:, 8 * P:8 * P + 4 * T2].rearrange("p (a b) -> p a b", a=4)
        at[0] = scratch0
        gn_d = room(4, T2)
        gn_s = room(4, T2)
        mid = room(4, TX)
        merged = room(8, TX)
        gate_s = room(2, 2, TX)
        part = room(2, 2, TX)
        at[0] = 0
        query = room(16, TX)
        score = room(2, 16, NE)
        best = room(16, TOPK)
        best_i = room(16, TOPK)
        best_u = carve(at[0], 16, TOPK).bitcast(U32)
        at[0] += 16 * TOPK
        cand = room(8, TOPK, TOPK)
        pick_k = room(2, 8, TOPK)
        pick_s = room(8, TOPK)
        pick_u = carve(at[0], 8, TOPK).bitcast(U32)
        at[0] += 8 * TOPK
        pick_hi_u = carve(at[0], 8, TOPK).bitcast(U32)
        at[0] += 8 * TOPK
        pick_lo_u = carve(at[0], 8, TOPK).bitcast(U32)
        at[0] += 8 * TOPK
        sel_eq = room(8, TOPK, TOPK)
        chosen = room(3, 2, 8, TOPK)
        soft = room(2, 8)
        chosen_t = sb("chosen_t", [P, 3, TX])
        key2 = sb("key2", [P, 2, 4])
        hot = sqf[:, 0:16 * P].rearrange("p (s k t n) -> p s k t n", s=2, k=2, t=4)
        gates_e = big[:, :].rearrange("p (e t) -> p e t", e=NE)
        act_e = sqf[:, 0:3 * TX].rearrange("p (a b) -> p a b", a=3)
        coef_e = sqf[:, 3 * TX:6 * TX].rearrange("p (a b) -> p a b", a=3)

        meta_loaded = sem("meta_loaded")
        pads_zeroed = sem("pads_zeroed")
        in2_copied = sem("in2_copied")
        glu_sig = sem("glu_sig")
        conv2_ready = sem("conv2_ready")
        shifted = sem("shifted")
        low_ready = sem("low_ready")
        up_sum = sem("up_sum")
        up_ready = sem("up_ready")
        kk_raw = sem("kk_raw")
        kk_squares = sem("kk_squares")
        kk_sum = sem("kk_sum")
        kk_mean = sem("kk_mean")
        kk_root = sem("kk_root")
        cums_ready = sem("cums_ready")
        cexp_ready = sem("cexp_ready")
        feats_ready = sem("feats_ready")
        bonus_in = sem("bonus_in")
        bonus_sum = sem("bonus_sum")
        tm_sum = sem("tm_sum")
        tm_ready = sem("tm_ready")
        gram_sum = sem("gram_sum")
        gram_ready = sem("gram_ready")
        mv_sum = sem("mv_sum")
        y_ready = sem("y_ready")
        pow_sum = sem("pow_sum")
        pow_ready = sem("pow_ready")
        app_sum = sem("app_sum")
        app_ready = sem("app_ready")
        eo_sum = sem("eo_sum")
        eo_ready = sem("eo_ready")
        spread_b = sem("spread_b")
        decay_diag = sem("decay_diag")
        fg_sum = sem("fg_sum")
        f_ready = sem("f_ready")
        g_ready = sem("g_ready")
        rec_sum = sem("rec_sum")
        state_ready = sem("state_ready")
        o_ready = sem("o_ready")
        cv_sum = sem("cv_sum")
        cv_mean = sem("cv_mean")
        cv_root = sem("cv_root")
        cv_out = sem("cv_out")
        gn_sum = sem("gn_sum")
        gn_sq = sem("gn_sq")
        gn_mean = sem("gn_mean")
        gn_root = sem("gn_root")
        mid_ready = sem("mid_ready")
        gate_sig = sem("gate_sig")
        merged_ready = sem("merged_ready")
        out2_added = sem("out2_added")
        q_copied = sem("q_copied")
        score_copied = sem("score_copied")
        pick_shift = sem("pick_shift")
        pick_exp = sem("pick_exp")
        chosen_ready = sem("chosen_ready")
        chosen_sum = sem("chosen_sum")
        chosen_turned = sem("chosen_turned")
        key2_ready = sem("key2_ready")
        hot_a = sem("hot_a")
        hot_b = sem("hot_b")
        gates_done = sem("gates_done")
        gates_copied = sem("gates_copied")
        expert_act = sem("expert_act")
        expert_coef = sem("expert_coef")
        cv_squares = sem("cv_squares")
        cv_diff = sem("cv_diff")
        spread_y = sem("spread_y")
        score_sum = sem("score_sum")
        out3_added = sem("out3_added")
        cv_scaled = sem("cv_scaled")

        def by_head(bank):
            return bank.rearrange("p (h t) -> p h t", h=4)


        stream = [(w1_in, Z1), (w1_cmp, 8), (w1_out, KD), (w1_ffn, 3 * NF)]
        stream += [(w2_in, 22), (w2_mid, 3 * KD), (w2_out, KD), (w2_q, 16), (w2_sub, 2), (experts, 2 * NE)]
        base, n = [], 0
        for _, count in stream:
            base.append(n)
            n += count
        NORMS = 7
        B_IN1, B_CMP, B_OUT1, B_FFN = base[:4]
        B_IN2, B_MID, B_OUT2, B_Q, B_SUB, B_EXP = base[4:]

        def landed(eng, b, k, i=None, per=RING):
            n = b + k
            v = 16 * (n // RING + 1)
            eng.wait_ge(tile_landed[n % RING], v if i is None else i * (16 * per // RING) + v)
            return ring[:, n % RING, :]

        block = ctx.enter_context(nc.Block())

        @block.sync
        def _(sp):
            sp.dma_start(hx1, x_t).then_inc(x_loaded, 16)
            sp.dma_start(hx[:, :, 0:N_META], meta_t).then_inc(meta_loaded, 16)
            sp.dma_start(cst[:], consts).then_inc(param_loaded, 16)
            sp.dma_start(col[:], cols).then_inc(param_loaded, 16)
            sp.dma_start(oh_tab[0:32, :], rel).then_inc(rel_loaded, 16)

            def load_tile(src, n, t, free):
                if free is not None:
                    sp.wait_ge(tiles_used, free)
                sp.dma_start(ring[:, n % RING, :], src[t]).then_inc(tile_landed[n % RING], 16)

            for (src, count), b in zip(stream, base):
                t0 = 0
                if b == 0:
                    for t in range(RING):
                        load_tile(src, t, t, None)
                    t0 = RING
                trips = (count - t0) // RING
                if trips > 1:
                    with sp.Fori(0, trips) as i:
                        for k in range(RING):
                            load_tile(src, b + t0 + k, i * RING + (t0 + k), i * RING + (b + t0 + k - RING + 1))
                    t0 += trips * RING
                for t in range(t0, count):
                    load_tile(src, b + t, t, b + t - RING + 1)

            sp.wait_ge(norm_out, NORMS)
            sp.dma_start(out_t, hn1).then_inc(out_stored, 16)
            sp.wait_ge(out_stored, 16)

        @block.gpsimd
        def _(pool):
            pool.memset(zeros[:], 0.0).then_inc(zeros_ready, 1)
            pool.wait_ge(zeros_ready, 1)
            pool.memset(oh_tab[32:33, :], NEG).then_inc(neg_row, 1)
            pool.wait_ge(brow_ready, 1)
            pool.dma_start(bias_rows, brow[0:N_HEADS, :]).then_inc(brow_stored, 16)
            pool.wait_ge(brow_stored, 16)
            rows = bias_rows.tensor

            pool.dma_start(bias_up, bass.AP(tensor=rows, offset=0, ap=[[1, P], [512, N_HEADS], [1, 3 * P]])).then_inc(bias_loaded, 16)

            pool.wait_ge(norm_out, 4)
            pool.memset(z2[:, :, 0:1], 0.0).then_inc(pads_zeroed, 1)
            pool.memset(glu[:, :, 0:TAPS - 1], 0.0).then_inc(pads_zeroed, 1)
            pool.wait_ge(feats_ready, 2)
            pool.wait_ge(cexp_ready, 5)
            pool.memset(state[:, :, 0, :], 0.0).then_inc(state_ready, 1)
            for tg in range(2):
                if tg > 0:
                    pool.wait_ge(o_ready, tg)
                pool.tensor_tensor(f_t, const("identhead").unsqueeze(1).unsqueeze(1).to_broadcast([P, 4, 8, HD]),
                                   chunk_decay[:, :, 8 * tg:8 * tg + 8].unsqueeze(3).to_broadcast([P, 4, 8, HD]),
                                   ALU.mult).then_inc(decay_diag, 1)
                for hh in range(2):
                    for p in range(2):
                        n = 4 * tg + 2 * hh + p
                        pool.wait_ge(app_ready, 4 * (2 * tg + hh + 1))
                        if n > 0:
                            pool.wait_ge(fg_sum, n)
                        for k, src in ((0, 3), (1, 1)):
                            a = (4 * hh + 2 * p) * HD
                            pool.tensor_tensor(expand[:, k], tm[:, src, a:a + P].rearrange("p (h k) -> p h k", h=2).unsqueeze(2).to_broadcast([P, 2, 8, HD]),
                                               const("chunk").unsqueeze(1).unsqueeze(3).to_broadcast([P, 2, 8, HD]),
                                               ALU.mult).then_inc(spread_b, 1)

            pool.wait_ge(chosen_turned, 3)
            with pool.Fori(0, TX // 8) as i:
                for s in range(2):
                    pool.wait_ge(gates_copied, i * 2 + (s + 1))
                    pool.tensor_copy(key2[:, s, :], chosen_t[:, 2, bass.ds(i * 8 + 4 * s, 4)]).then_inc(key2_ready, 1)
                    pool.wait_ge(chosen_turned, 3)
                    pool.wait_ge(key2_ready, i * 2 + (s + 1))
                    for t in range(4):
                        ins = pool.tensor_scalar(hot[:, s, 1, t, :], const("iota"), key2[:, s, t:t + 1], None, ALU.is_equal)
                    ins.then_inc(hot_b, 1)

        @block.tensor
        def _(pe):
            def norm_pe(n, width, bank):
                pe.wait_ge(norm_squares, n + 1)
                for k in range(KD):
                    mm = pe.matmul(psum[:, bank, 0:width], const("ones"), sq[:, k, 0:width],
                                   start=(k == 0), stop=(k == KD - 1))
                mm.then_inc(norm_sums, 1)

            def project(tile, dst, width, src=None):
                src = hn if src is None else src
                for k in range(KD):
                    mm = pe.matmul(dst, tile[:, k * P:(k + 1) * P], src[:, k, 0:width],
                                   start=(k == 0), stop=(k == KD - 1))
                return mm

            def zero_y():
                for m in range(4):
                    pe.matmul(psum[:, 4 + m, :], zeros[:], cst[:, 0:512], start=True, stop=False, skip_group_check=True)

            pe.wait_ge(param_loaded, 32)
            pe.wait_ge(rel_loaded, 16)
            pe.wait_ge(neg_row, 1)
            pe.matmul(psum[0:N_HEADS, 7, :], oh_tab[0:33, :], const("onehot")[0:33, :],
                      start=True, stop=True).then_inc(brow_sum, 1)

            norm_pe(0, TX, 6)
            pe.wait_ge(norm_out, 1)
            for qt in range(2):
                for k in range(KD):
                    mm = pe.matmul(psum[:, 6, qt * 24:(qt + 1) * 24], hn[:, k, qt * P:(qt + 1) * P],
                                   colv("gates", k * 24, (k + 1) * 24), start=(k == 0), stop=(k == KD - 1))
            mm.then_inc(gates_sum, 1)
            with pe.Fori(0, Z1 // RING) as i:
                for k in range(RING):
                    tile = landed(pe, B_IN1, k, i)
                    pe.wait_ge((in1_even, in1_odd)[k % 2], i * 3 + (k // 2 + 1))
                    project(tile, psum[:, k, 0:TX], TX).then_inc(tiles_used, 1)

            for kv in range(2):
                pe.wait_ge(cmp_blocks, 1)
                for j in range(4):
                    tile = landed(pe, B_CMP, kv * 4 + j)
                    for r in range(4):
                        for c in range(2):
                            mm = pe.matmul(psum[:, 2 * kv + c, 0:2 * N_CMP], tile[:, (r * 2 + c) * P:(r * 2 + c + 1) * P],
                                           cmp_in[:, kv, 4 * j + r, :], start=(j + r == 0), stop=(j + r == 6))
                    mm.then_inc(tiles_used, 1)
            for b, zt in enumerate((ZVS, ZVW)):
                for kt in range(2):
                    mm = pe.transpose(psum[:, 4, (b * 2 + kt) * P:(b * 2 + kt + 1) * P],
                                      z1[:, zt, kt * P:(kt + 1) * P], const("ident"))
            mm.then_inc(vtok_sum, 1)
            pe.wait_ge(cmp_hid_ready, 4)
            for c in range(2):
                pe.matmul(psum[:, 5, 0:2 * N_CMP], colv("w2k", c * P, (c + 1) * P), cmp_hid[:, 0, c, :],
                          start=(c == 0), stop=(c == 1))
            for g in range(N_KV):
                for c in range(2):
                    mm = pe.matmul(psum[0:N_CMP, 5, 64 + g * HD:64 + (g + 1) * HD],
                                   cmp_hid[:, 1, c, g * N_CMP:(g + 1) * N_CMP], colv("w2v", c * HD, (c + 1) * HD),
                                   start=(c == 0), stop=(c == 1))
            mm.then_inc(cmp_sum, 1)

            pe.wait_ge(bias_loaded, 16)
            pe.wait_ge(gates_ready, 1)
            pe.wait_ge(brow_ready, 1)
            for n in range(6):
                pe.matmul(psum[:, BIAS_BANKS[n], :], const("flip"), mix_y[:, n * 512:(n + 1) * 512],
                          start=True, stop=True).then_inc(bias_turned, 1)

            batches = [0]

            def logits(gi):
                qt, g = gi // 2, gi % 2
                half = slice(g * HD, (g + 1) * HD)
                nk = P * (qt + 1)
                for b, kt in enumerate((ZKS, ZKW)):
                    if gi > 0:
                        pe.wait_ge(logits_ready, 3 * (gi - 1) + b + 1)
                    for i in range(REP):
                        mm = pe.matmul(psum[:, 2 * b + i // 2, (i % 2) * TX:(i % 2) * TX + nk],
                                       z1[half, ZQ + i, qt * P:(qt + 1) * P], z1[half, kt, 0:nk], start=True, stop=True)
                    mm.then_inc(logits_sum, 1)
                if gi == 0:
                    pe.wait_ge(cmp_ready, 3)
                    pe.wait_ge(vtok_ready, 1)
                else:
                    pe.wait_ge(logits_ready, 3 * gi)
                for i in range(REP):
                    mm = pe.matmul(psum[:, 4, i * 16:i * 16 + N_CMP], z1[half, ZQ + i, qt * P:(qt + 1) * P],
                                   k_cmp[half, :], start=True, stop=True)
                mm.then_inc(logits_sum, 1)

            def turn(gi, b, src, rows):
                bank = 5 + batches[0] % 2
                if batches[0] >= 2:
                    pe.wait_ge(turned_copied, batches[0] - 1)
                for i in range(REP):
                    mm = pe.transpose(psum[0:rows, bank, i * P:(i + 1) * P], src(i), const("ident"))
                mm.then_inc(turned, 1)
                batches[0] += 1

            def attend(gi):
                qt, g = gi // 2, gi % 2
                for b in range(2):
                    pe.wait_ge(probs_ready, 3 * gi + b + 1)
                    for kt in range(qt + 1):
                        turn(gi, b, lambda i: zbuf[:, b, i, kt * P:(kt + 1) * P], P)
                pe.wait_ge(probs_ready, 3 * gi + 3)
                turn(gi, 2, lambda i: zbuf_c[:, i, :], N_CMP)
                pe.wait_ge(turned_copied, batches[0])
                if gi > 0:
                    pe.wait_ge(heads_ready, gi)
                else:
                    pe.wait_ge(brow_ready, 1)
                dst = psum[g * HD:(g + 1) * HD, 7, :]
                n = 0
                for b in range(2):
                    for kt in range(qt + 1):
                        pe.matmul(dst, v_tok[:, b, kt, g * HD:(g + 1) * HD], probs_t[:, gi % 2, n, :],
                                  start=(n == 0), stop=False)
                        n += 1
                pe.matmul(dst, v_cmp[0:N_CMP, g * HD:(g + 1) * HD], probs_t[0:N_CMP, gi % 2, n, :],
                          start=False, stop=True).then_inc(heads_sum, 1)

            pe.wait_ge(in1_even, 3 + Z1 // 2)
            pe.wait_ge(in1_odd, 3 + Z1 // 2)
            pe.wait_ge(bias_ready, 6)
            logits(0)
            for gi in range(4):
                if gi < 3:
                    logits(gi + 1)
                attend(gi)

            pe.wait_ge(heads_ready, 4)
            pe.wait_ge(conv_ready, 1)
            for m in range(KD):
                tile = landed(pe, B_OUT1, m)
                if m >= 4:
                    pe.wait_ge(out1_ready, m - 3)
                project(tile, psum[:, m % 4, 0:TX], TX, mix).then_inc(tiles_used, 1)
            norm_pe(1, TX, 4)
            norm_pe(2, TX, 5)

            pe.wait_ge(norm_out, 3)
            pe.wait_ge(zeros_ready, 1)
            zero_y()

            def ffn_up(j, k0, i=None):
                for half in range(2):
                    tile = landed(pe, B_FFN, k0 + half, i)
                    bank = 2 * (j % 2) + half
                    if i is not None:
                        pe.wait_ge((ffn_conv_g, ffn_conv_u)[half], i * 2 + (j + 1))
                    else:
                        pe.wait_ge((ffn_conv_g, ffn_conv_u)[half], j + 1)
                    project(tile, psum[:, bank, 0:TX], TX).then_inc(tiles_used, 1)

            def down(tile, h):
                for m in range(KD):
                    mm = pe.matmul(psum[:, 4 + m // 2, (m % 2) * TX:(m % 2 + 1) * TX], tile[:, m * P:(m + 1) * P], h,
                                   start=False, stop=False, skip_group_check=True)
                return mm

            def ffn_down(j, k0, i=None):
                tile = landed(pe, B_FFN, k0, i)
                pe.wait_ge(ffn_hidden, j + 1 if i is None else i * 2 + (j + 1))
                return down(tile, ffn_h[:, j % 2, :])

            ffn_up(0, 0)
            with pe.Fori(0, (NF - 2) // 2) as i:
                for s in range(2):
                    ffn_up(s + 1, 2 + 3 * s, i)
                    ffn_down(s, 4 + 3 * s, i).then_inc(tiles_used, 1)
            ffn_up(NF - 1, 3 * NF - 4)
            ffn_down(NF - 2, 3 * NF - 2).then_inc(tiles_used, 1)
            ffn_down(NF - 1, 3 * NF - 1).then_inc(tiles_used, 1)
            norm_pe(3, TX, 0)

            norm_pe(4, T2, 7)
            pe.wait_ge(norm_out, 5)
            def in2(k, i=None):
                tile = landed(pe, B_IN2, k, i)
                pe.wait_ge(in2_copied, k + 1 if i is None else i * RING + (k + 1))
                project(tile, psum[:, k % RING, 0:T2], T2).then_inc(tiles_used, 1)

            with pe.Fori(0, 3) as i:
                for k in range(RING):
                    in2(k, i)
            for k in range(18, 22):
                in2(k)

            for r in range(2):
                pe.wait_ge((conv2_ready, cv_squares)[r], 1)
                for k in range(4):
                    mm = pe.matmul(psum[:, 6, 0:T2], const("ones"), (conv_y, sq4)[r][:, k, :], start=(k == 0), stop=(k == 3))
                mm.then_inc(cv_sum, 1)

            pe.wait_ge(in2_copied, RING + 22)
            for n, (lo, hi, w, src) in enumerate(((0, HD, "wa_up", 20), (HD, P, "wa_up", 20), (0, P, "g_up", 21))):
                pe.wait_ge(low_ready, 2)
                for m in range(4):
                    if n == 2:
                        pe.wait_ge(up_ready, m + 1)
                    if n == 1 and m == 2:
                        pe.wait_ge(cv_mean, 2)
                    mm = pe.matmul(psum[:, (4 * n + m) % 8, 0:T2], colv(w, m * P, (m + 1) * P)[lo:hi], z2[lo:hi, src, 1:T2 + 1],
                                   start=True, stop=True)
                    mm.then_inc(up_sum, 1)
            for r, (ready, src) in enumerate(((kk_squares, sq4), (bonus_in, sq4))):
                pe.wait_ge(ready, 1)
                if r == 0:
                    pe.wait_ge(up_ready, 8)
                for m in range(4):
                    mm = pe.matmul(psum[:, 4 + m, 0:T2], const("headones"), src[:, m, :], start=True, stop=True)
                mm.then_inc((kk_sum, bonus_sum)[r], 1)

            pe.wait_ge(up_ready, 12)
            pe.wait_ge(feats_ready, 2)

            def fm(x, h, t0, nt):
                q = slice(h % 2 * HD, (h % 2 + 1) * HD)
                return x[q, h // 2, t0:t0 + nt]

            for tg in range(3):
                t0, nt = tg * P, min(P, T2 - tg * P)
                if tg > 0:
                    pe.wait_ge(o_ready, tg)
                for n, src in enumerate((alpha, z2[:, 16:20, 1:T2 + 1], kappa_end, beta_end)):
                    for m in range(4):
                        mm = pe.transpose(psum[0:nt, n, m * P:(m + 1) * P], src[:, m, t0:t0 + nt], const("ident"))
                    mm.then_inc(tm_sum, 1)
                for hh in range(2):
                    u = 2 * tg + hh
                    pe.wait_ge(tm_ready, 4 * (tg + 1))
                    if u > 0:
                        pe.wait_ge(eo_ready, 2 * u)
                        pe.wait_ge(f_ready, min(2 * u, 8))
                        pe.wait_ge(g_ready, min(2 * u, 8))
                    G = lambda n, h: gram[0:nt, n, h, 0:nt]
                    yh = lambda h, a=0, b=P: ycol[0:nt, h, a:b]
                    tmh = lambda n, h: tm[0:nt, n, (4 * hh + h) * HD:(4 * hh + h + 1) * HD]
                    out = lambda bank, h: psum[0:nt, bank, h * P:h * P + nt]
                    for n, kinds in enumerate((((beta, alpha), (kappa, alpha)), ((alpha, beta),), ((beta, rho), (kappa, rho)))):
                        for odd in range(2):
                            for k, (x, y) in enumerate(kinds):
                                for h in (odd, odd + 2):
                                    mm = pe.matmul(out(2 * n + odd, 2 * k + h // 2), fm(x, 4 * hh + h, t0, nt),
                                                   fm(y, 4 * hh + h, t0, nt), start=True, stop=True)
                            mm.then_inc(gram_sum, 1)

                    def product(bank, a, b, done, rhs=None):
                        for h in range(4):
                            r = G(b, h) if rhs is None else rhs(h)
                            dst = psum[0:nt, bank, h * P:h * P + r.shape[1]]
                            mm = pe.matmul(dst, G(a, h), r, start=True, stop=True)
                        mm.then_inc(done, 1)

                    pe.wait_ge(gram_ready, 6 * u + 4)
                    product(6, G_LT, G_L, pow_sum)
                    product(7, G_L, G_LT, pow_sum)
                    product(1, G_MT, None, mv_sum, lambda h: tmh(1, h))
                    pe.wait_ge(y_ready, 2 * u + 2)
                    product(0, G_LT, None, app_sum, yh)
                    pe.wait_ge(pow_ready, 5 * u + 2)
                    product(2, G_L2T, G_L2, pow_sum)
                    product(3, G_L2, G_L2T, pow_sum)
                    pe.wait_ge(app_ready, 4 * u + 1)
                    product(1, G_L2T, None, app_sum, yh)
                    pe.wait_ge(pow_ready, 5 * u + 4)
                    product(6, G_L4, G_L4T, pow_sum)
                    pe.wait_ge(app_ready, 4 * u + 2)
                    product(0, G_L4T, None, app_sum, yh)
                    pe.wait_ge(pow_ready, 5 * u + 5)
                    pe.wait_ge(app_ready, 4 * u + 3)
                    product(1, G_L8T, None, app_sum, yh)
                    pe.wait_ge(app_ready, 4 * u + 4)
                    pe.wait_ge(gram_ready, 6 * u + 6)
                    for h in range(4):
                        q = slice(h % 2 * HD, (h % 2 + 1) * HD)
                        c = h // 2 * P
                        pe.matmul(psum[q, 4, c:c + nt], yh(h, 0, HD), G(G_QT, h), start=True, stop=True)
                        pe.matmul(psum[q, 5, c:c + nt], tmh(1, h), G(G_RT, h), start=True, stop=False)
                        mm = pe.matmul(psum[q, 5, c:c + nt], yh(h, HD, P), G(G_QT, h), start=False, stop=True)
                    mm.then_inc(eo_sum, 1)
                    if tg < 2:
                        for p in range(2):
                            n = 2 * u + p
                            pe.wait_ge(spread_b, 2 * (n + 1))
                            pe.wait_ge(spread_y, n + 1)
                            if p > 0:
                                pe.wait_ge(f_ready, n)
                                pe.wait_ge(g_ready, n)
                            for x in range(2):
                                h = 2 * p + x
                                q = slice(x * HD, (x + 1) * HD)
                                ex = lambda k: expand[0:nt, k, x].rearrange("p a b -> p (a b)")
                                pe.matmul(psum[q, 6, :], yh(h, 0, HD), ex(0), start=True, stop=True)
                                pe.matmul(psum[q, 7, :], tmh(2, h), ex(1), start=True, stop=False)
                                mm = pe.matmul(psum[q, 7, :], tmh(3, h), ex(2), start=False, stop=True)
                            mm.then_inc(fg_sum, 1)
                if tg < 2:
                    pe.wait_ge(f_ready, 4 * (tg + 1))
                    pe.wait_ge(g_ready, 4 * (tg + 1))
                pe.wait_ge(eo_ready, 4 * (tg + 1))
                for c in range(nt // CH):
                    slot = 8 if tg and c == 0 else c
                    pe.wait_ge(state_ready, 8 * tg + c + 1)
                    for h in range(8):
                        q = slice(h % 2 * HD, (h % 2 + 1) * HD)
                        s = state[q, h // 2, slot, :]
                        mm = pe.matmul(psum[q, 2, h // 2 * P + c * CH:h // 2 * P + (c + 1) * CH], s,
                                       e_t[q, h // 2, c * CH:(c + 1) * CH], start=True, stop=True)
                    if tg < 2:
                        for h in range(8):
                            q = slice(h % 2 * HD, (h % 2 + 1) * HD)
                            mm = pe.matmul(psum[q, c % 2, h // 2 * HD:(h // 2 + 1) * HD], f_t[q, h // 2, c, :],
                                           state[q, h // 2, slot, :], start=True, stop=True)
                    mm.then_inc(rec_sum, 1)

            for r in range(2):
                if r == 0:
                    pe.wait_ge(o_ready, 3)
                else:
                    pe.wait_ge(gn_sq, 1)
                for m in range(4):
                    mm = pe.matmul(psum[:, 4 * r + m, 0:T2], const("headones"), (o_all, gn_s)[r][:, m, :], start=True, stop=True)
                mm.then_inc(gn_sum, 1)

            pe.wait_ge(mid_ready, 1)
            pe.wait_ge(cv_out, 4)
            for m in range(KD):
                if m >= 2:
                    pe.wait_ge(merged_ready, m - 1)
                b0 = 4 * (m % 2)
                for n in range(2):
                    tile = landed(pe, B_MID, 3 * m + n)
                    project(tile, psum[:, b0 + n, 0:TX], TX, hn[:, :, N_META:T2]).then_inc(tiles_used, 1)
                tile = landed(pe, B_MID, 3 * m + 2)
                for k in range(8):
                    mm = pe.matmul(psum[:, b0 + 2 + k // 4, 0:TX], tile[:, k * P:(k + 1) * P],
                                   conv_y[:, k, N_META:T2] if k < 4 else mid[:, k - 4, :],
                                   start=(k % 4 == 0), stop=(k % 4 == 3))
                mm.then_inc(tiles_used, 1)
            pe.wait_ge(merged_ready, KD)
            for m in range(KD):
                tile = landed(pe, B_OUT2, m)
                project(tile, psum[:, m, 0:TX], TX, merged).then_inc(tiles_used, 1)
            pe.wait_ge(out2_added, KD)
            norm_pe(5, TX, 6)
            pe.wait_ge(norm_out, 6)

            for m in range(16):
                tile = landed(pe, B_Q, m)
                if m >= 4:
                    pe.wait_ge(q_copied, m - 3)
                project(tile, psum[:, m % 4, 0:TX], TX).then_inc(tiles_used, 1)
            for n in range(2):
                tile = landed(pe, B_SUB, n)
                if n == 0:
                    pe.wait_ge(q_copied, 16)
                for qt in range(2):
                    if n == 1:
                        pe.wait_ge(score_copied, 2 * qt + 2)
                    for k in range(8):
                        mm = pe.matmul(psum[:, 4 * qt + k // 4 + 0, (k % 4) * P:(k % 4 + 1) * P],
                                       query[:, 8 * n + k, qt * P:(qt + 1) * P], tile[:, k * P:(k + 1) * P], start=True, stop=True)
                        if k % 4 == 3 and not (qt == 1 and k == 7):
                            mm.then_inc(score_sum, 1)
                mm.then_inc(tiles_used, 1)

            for qt in range(2):
                pe.wait_ge(chosen_ready, qt + 1)
                for n in range(3):
                    mm = pe.transpose(psum[:, n, qt * P:(qt + 1) * P], chosen[:, n, qt].rearrange("p a b -> p (a b)"), const("ident"))
            mm.then_inc(chosen_sum, 1)

            pe.wait_ge(chosen_turned, 3)
            with pe.Fori(0, TX // 8) as i:
                for s in range(2):
                    pe.wait_ge(hot_a, i * 2 + (s + 1))
                    pe.wait_ge(hot_b, i * 2 + (s + 1))
                    pe.wait_ge(gates_copied, i * 2 + (s + 1))
                    for t in range(4):
                        mm = pe.matmul(psum[:, s, t * P:(t + 1) * P], hot[:, s, 0, t, :], hot[:, s, 1, t, :], start=True, stop=True)
                    mm.then_inc(gates_done, 1)

            pe.wait_ge(gates_copied, 2 + TX // 4)
            zero_y()

            def expert_up(e, i=None):
                tile = landed(pe, B_EXP, max(2 * e - 1, 0), i)
                pe.wait_ge(expert_act, e + 1 if i is None else i * 3 + (e + 1))
                project(tile, psum[:, e % 3, 0:TX], TX).then_inc(tiles_used, 1)

            def expert_down(e, i=None):
                tile = landed(pe, B_EXP, 2 * e + 2 if e < NE - 1 else 2 * NE - 1, i)
                pe.wait_ge(expert_coef, e + 1 if i is None else i * 3 + (e + 1))
                down(tile, coef_e[:, e % 3, :]).then_inc(tiles_used, 1)

            expert_up(0)
            with pe.Fori(0, (NE - 1) // 3) as i:
                for s in range(3):
                    expert_up(s + 1, i)
                    expert_down(s, i)
            expert_up(NE - 1)
            expert_down(NE - 2)
            expert_down(NE - 1)
            norm_pe(6, TX, 0)

        @block.scalar
        def _(act):
            def norm_act(n, src, width, ready):
                ready()
                act.activation(sq[:, :, 0:width], src, ACT.Square).then_inc(norm_squares, 1)

            def norm_root_act(n, width):
                act.wait_ge(norm_mean, n + 1)
                act.activation(rms[:, 0, 0:width], rms[:, 0, 0:width], ACT.Sqrt).then_inc(norm_root, 1)

            norm_act(0, hx1, TX, lambda: act.wait_ge(x_loaded, 16))
            norm_root_act(0, TX)
            act.sem_inc(in1_odd, 3)
            with act.Fori(0, Z1 // RING) as i:
                for k in (1, 3, 5):
                    act.wait_ge(tiles_used, i * RING + (B_IN1 + k + 1))
                    act.activation(z1[:, i * RING + k, :], psum[:, k, 0:TX], ACT.Copy).then_inc(in1_odd, 1)
            act.wait_ge(gates_sum, 1)
            act.activation(gates, psum[:, 6, 0:48].rearrange("p (a b) -> p a b", a=2), ACT.Sigmoid).then_inc(gates_ready, 1)
            for kv in range(2):
                act.wait_ge(tiles_used, B_CMP + 4 * (kv + 1))
                for c in range(2):
                    act.activation(cmp_hid[:, kv, c, :], psum[:, 2 * kv + c, 0:2 * N_CMP],
                                   ACT.Gelu_apprx_tanh).then_inc(cmp_hid_ready, 1)

            for n in range(6):
                act.wait_ge(bias_turned, n + 1)
                act.activation(bias_t.rearrange("p h k -> p (h k)")[:, n * 512:(n + 1) * 512], psum[:, BIAS_BANKS[n], :],
                               ACT.Copy).then_inc(bias_ready, 1)

            batches = [0]
            for gi in range(4):
                qt, g = gi // 2, gi % 2
                nk = P * (qt + 1)
                for b in range(2):
                    act.wait_ge(logits_ready, 3 * gi + b + 1)
                    act.activation(zbuf[:, b, :, 0:nk], zbuf[:, b, :, 0:nk], ACT.Exp).then_inc(exps_ready, 1)
                act.wait_ge(logits_ready, 3 * gi + 3)
                act.activation(zbuf_c, zbuf_c, ACT.Exp).then_inc(exps_ready, 1)
                if gi >= 2:
                    act.wait_ge(heads_sum, gi - 1)
                for n in range(2 * (qt + 1) + 1):
                    rows = N_CMP if n == 2 * (qt + 1) else P
                    act.wait_ge(turned, batches[0] + 1)
                    act.activation(probs_t[0:rows, gi % 2, n, :], psum[0:rows, 5 + batches[0] % 2, :],
                                   ACT.Copy).then_inc(turned_copied, 1)
                    batches[0] += 1
                act.wait_ge(heads_sum, gi + 1)
                half = slice(g * HD, (g + 1) * HD)
                act.activation(mix[half, 0:REP, qt * P:(qt + 1) * P],
                               psum[half, 7, :].rearrange("p (a b) -> p a b", a=REP), ACT.Copy).then_inc(heads_ready, 1)

            for m in range(KD):
                act.wait_ge(tiles_used, B_OUT1 + m + 1)
                act.activation(y1[:, m, :], psum[:, m % 4, 0:TX], ACT.Copy).then_inc(out1_ready, 1)
            norm_act(1, y1, TX, lambda: act.wait_ge(out1_ready, KD))
            norm_root_act(1, TX)
            norm_act(2, hx1, TX, lambda: act.wait_ge(norm_out, 2))
            norm_root_act(2, TX)

            def ffn_act(j, i=None):
                def trips(per, v):
                    return v if i is None else i * per + v

                par = j % 2
                act.wait_ge(ffn_taps, trips(2, j + 1))
                for half in range(2):
                    act.wait_ge(tiles_used, trips(RING, B_FFN + (3 * j + half if j else half + 1)))
                    act.activation(ffn_c[:, par, half, :], psum[:, 2 * par + half, 0:TX], ACT.Copy,
                                   scale=taps[:, par, 3 * half + 2:3 * half + 3]).then_inc(ffn_scaled, 1)
                act.wait_ge(ffn_conv_g, trips(2, j + 3))
                act.activation(ffn_g[:, par, :], ffn_c[:, par, 0, :], ACT.Gelu_apprx_tanh).then_inc(ffn_gelu, 1)

            ffn_act(0)
            with act.Fori(0, (NF - 2) // 2) as i:
                ffn_act(1, i)
                ffn_act(2, i)
            ffn_act(NF - 1)
            act.wait_ge(tiles_used, B_FFN + 3 * NF)
            for m in range(4):
                act.activation(y1[:, 2 * m:2 * m + 2, :], psum[:, 4 + m, :].rearrange("p (a b) -> p a b", a=2),
                               ACT.Copy).then_inc(ffn_copied, 1)
            norm_act(3, y1, TX, lambda: act.wait_ge(ffn_copied, 4))
            norm_root_act(3, TX)

            norm_act(4, hx[:, :, :], T2, lambda: (act.wait_ge(meta_loaded, 16), act.wait_ge(norm_out, 4)))
            norm_root_act(4, T2)
            act.wait_ge(pads_zeroed, 2)
            act.sem_inc(in2_copied, RING)
            with act.Fori(0, 2) as i:
                for k in range(RING):
                    act.wait_ge(tiles_used, i * RING + (B_IN2 + k + 1))
                    act.activation(z2[:, i * RING + k, 1:T2 + 1], psum[:, k, 0:T2], ACT.Copy).then_inc(in2_copied, 1)
            act.wait_ge(in2_copied, RING + 12)
            act.activation(z2[:, 4:8, 1:T2 + 1], z2[:, 4:8, 1:T2 + 1], ACT.Sigmoid).then_inc(glu_sig, 1)
            for k in range(12, 22):
                act.wait_ge(tiles_used, B_IN2 + k + 1)
                act.activation(z2[:, k, 1:T2 + 1], psum[:, k % RING, 0:T2], ACT.Copy).then_inc(in2_copied, 1)

            act.wait_ge(cv_diff, 1)
            act.activation(sq4, conv_y, ACT.Square).then_inc(cv_squares, 1)
            act.wait_ge(cv_mean, 2)
            act.activation(rms[:, 0, :], rms[:, 0, :], ACT.Sqrt).then_inc(cv_root, 1)
            act.wait_ge(cv_scaled, 1)
            for m in range(4):
                act.activation(conv_y[:, m, :], conv_y[:, m, :], ACT.Silu, scale=colv("ln_g", m, m + 1),
                               bias=colv("ln_b", m, m + 1)).then_inc(cv_out, 1)

            act.wait_ge(shifted, 1)
            act.activation(z2[0:HD, 20, 1:T2 + 1], z2[0:HD, 20, 1:T2 + 1], ACT.Tanh).then_inc(low_ready, 1)
            act.activation(z2[:, 21, 1:T2 + 1], z2[:, 21, 1:T2 + 1], ACT.Sigmoid).then_inc(low_ready, 1)
            for n, (dst, b) in enumerate(((logdec, "w0"), (a_gate, "a0"))):
                for m in range(4):
                    act.wait_ge(up_sum, 4 * n + m + 1)
                    act.activation(dst[:, m, :], psum[:, 4 * n + m, 0:T2], ACT.Sigmoid,
                                   bias=colv(b, m, m + 1)).then_inc(up_ready, 1)
            act.wait_ge(kk_raw, 1)
            act.activation(sq4, kk, ACT.Square).then_inc(kk_squares, 1)
            for m in range(4):
                act.wait_ge(up_sum, 9 + m)
                act.activation(gmul[:, m, :], psum[:, m, 0:T2], ACT.Copy).then_inc(up_ready, 1)
            act.wait_ge(kk_mean, 1)
            act.activation(k_new, k_new, ACT.Sqrt).then_inc(kk_root, 1)
            act.wait_ge(cums_ready, 1)
            act.activation(e_cum, cum, ACT.Exp).then_inc(cexp_ready, 1)
            act.activation(e_neg, cum, ACT.Exp, scale=-1.0).then_inc(cexp_ready, 1)
            act.activation(e_prev, e_prev, ACT.Exp).then_inc(cexp_ready, 1)
            act.activation(e_end, e_end, ACT.Exp).then_inc(cexp_ready, 1)
            act.activation(chunk_decay, cum[:, :, CH - 1:T2:CH], ACT.Exp).then_inc(cexp_ready, 1)

            for tg in range(3):
                nt = min(P, T2 - tg * P)
                for n in range(4):
                    act.wait_ge(tm_sum, 4 * tg + n + 1)
                    act.activation(tm[0:nt, n, :], psum[0:nt, n, :], ACT.Copy).then_inc(tm_ready, 1)
                for hh in range(2):
                    u = 2 * tg + hh

                    def power(k, bank, dst):
                        act.wait_ge(pow_sum, 5 * u + k)
                        act.activation(gram[0:nt, dst, :, 0:nt], by_head(psum[0:nt, bank, :])[:, :, 0:nt],
                                       ACT.Copy).then_inc(pow_ready, 1)

                    act.wait_ge(mv_sum, u + 1)
                    act.activation(ycol[0:nt, :, 0:HD], tm[0:nt, 0, 4 * hh * HD:4 * (hh + 1) * HD].rearrange("p (h k) -> p h k", h=4),
                                   ACT.Copy).then_inc(y_ready, 1)
                    act.activation(ycol[0:nt, :, HD:P], by_head(psum[0:nt, 1, :])[:, :, 0:HD], ACT.Copy).then_inc(y_ready, 1)
                    power(1, 6, G_L2)
                    power(2, 7, G_L2T)
                    power(3, 2, G_L4)
                    power(4, 3, G_L4T)
                    power(5, 6, G_L8T)
                    if tg < 2:
                        for p in range(2):
                            act.wait_ge(fg_sum, 2 * u + p + 1)
                            act.activation(g_c[:, 2 * hh + p].rearrange("p a b -> p (a b)"), psum[:, 7, :],
                                           ACT.Copy).then_inc(g_ready, 1)

            act.wait_ge(gn_mean, 1)
            act.activation(gn_s, gn_s, ACT.Sqrt).then_inc(gn_root, 1)
            for m in range(KD):
                act.wait_ge(tiles_used, B_MID + 3 * m + 2)
                act.activation(gate_s[:, m % 2], psum[:, 4 * (m % 2):4 * (m % 2) + 2, 0:TX], ACT.Sigmoid).then_inc(gate_sig, 1)
            norm_act(5, hx1, TX, lambda: act.wait_ge(out2_added, KD))
            norm_root_act(5, TX)

            for m in range(16):
                act.wait_ge(tiles_used, B_Q + m + 1)
                act.activation(query[:, m, :], psum[:, m % 4, 0:TX], ACT.Copy).then_inc(q_copied, 1)
            for n in range(2):
                for qt in range(2):
                    for b in range(2):
                        if qt + b == 2:
                            act.wait_ge(tiles_used, B_SUB + n + 1)
                        else:
                            act.wait_ge(score_sum, 3 * n + 2 * qt + b + 1)
                        act.activation(score[:, qt, 8 * n + 4 * b:8 * n + 4 * b + 4, :].rearrange("p a b -> p (a b)"),
                                       psum[:, 4 * qt + b, :], ACT.Copy).then_inc(score_copied, 1)
            for qt in range(2):
                act.wait_ge(pick_shift, qt + 1)
                act.activation(pick_s, pick_s, ACT.Exp).then_inc(pick_exp, 1)

            act.wait_ge(chosen_turned, 3)
            act.sem_inc(gates_copied, 2)
            with act.Fori(0, TX // 8) as i:
                for s in range(2):
                    act.wait_ge(gates_done, i * 2 + (s + 1))
                    act.activation(gates_e[:, :, bass.ds(i * 8 + 4 * s, 4)].rearrange("p e t -> p t e"),
                                   psum[:, s, :].rearrange("p (t e) -> p t e", t=4), ACT.Copy).then_inc(gates_copied, 1)

            act.sem_inc(expert_act, 3)

            def expert(e, i=None):
                n = B_EXP + max(2 * e, 1)
                act.wait_ge(tiles_used, n if i is None else i * RING + n)
                act.activation(act_e[:, e % 3, :], psum[:, e % 3, 0:TX], ACT.Gelu).then_inc(expert_act, 1)

            expert(0)
            with act.Fori(0, (NE - 1) // 3) as i:
                for s in range(1, 4):
                    expert(s, i)
            expert(NE - 1)
            norm_act(6, hx1, TX, lambda: act.wait_ge(out3_added, 4))
            norm_root_act(6, TX)

        @block.vector
        def _(dve):
            steps = [0]

            def step(ins):
                steps[0] += 1
                ins.then_inc(dve_step, 1)
                dve.wait_ge(dve_step, steps[0])

            def norm_scale(n, width, bank, total=D, eps=EPS):
                dve.wait_ge(norm_sums, n + 1)
                dve.tensor_scalar(rms[:, 0, 0:width], psum[:, bank, 0:width], 1.0 / total, eps,
                                  ALU.mult, ALU.add).then_inc(norm_mean, 1)
                dve.wait_ge(norm_root, n + 1)
                step(dve.reciprocal(rms[:, 1, 0:width], rms[:, 0, 0:width]))

            def norm_pre(n, src, width, bank, gain):
                norm_scale(n, width, bank)
                for k in range(KD):
                    ins = dve.scalar_tensor_tensor(out=hn[:, k, 0:width], in0=src[:, k, :], scalar=colv(gain, k, k + 1),
                                                   in1=rms[:, 1, 0:width], op0=ALU.mult, op1=ALU.mult)
                ins.then_inc(norm_out, 1)

            def norm_post(n, y, width, bank, gain):
                norm_scale(n, width, bank)
                step(dve.tensor_tensor(y, y, rms[:, 1, 0:width].unsqueeze(1).to_broadcast([P, KD, width]), ALU.mult))
                for k in range(KD):
                    ins = dve.scalar_tensor_tensor(out=hx1[:, k, :], in0=y[:, k, :], scalar=colv(gain, k, k + 1),
                                                   in1=hx1[:, k, :], op0=ALU.mult, op1=ALU.add)
                ins.then_inc(norm_out, 1)

            dve.wait_ge(brow_sum, 1)
            dve.tensor_copy(brow[0:N_HEADS, :], psum[0:N_HEADS, 7, :]).then_inc(brow_ready, 1)
            dve.wait_ge(param_loaded, 32)
            dve.wait_ge(x_loaded, 16)
            norm_pre(0, hx1, TX, 6, "mix_pre")
            dve.sem_inc(in1_even, 3)
            with dve.Fori(0, Z1 // RING) as i:
                for k in (0, 2, 4):
                    dve.wait_ge(tiles_used, i * RING + (B_IN1 + k + 1))
                    dve.tensor_copy(z1[:, i * RING + k, :], psum[:, k, 0:TX]).then_inc(in1_even, 1)
            dve.wait_ge(in1_odd, 3 + Z1 // 2)
            dve.wait_ge(in1_even, 3 + Z1 // 2)

            for kv in range(2):
                for g in range(N_KV):
                    for half in range(2):
                        q = slice(half * HD, (half + 1) * HD)
                        src = z1[q, ZKC + 2 * kv + g, half * 16:half * 16 + 16 * N_CMP].rearrange("p (n r) -> p r n", r=16)
                        ins = dve.tensor_tensor(cmp_in[q, kv, :, g * N_CMP:(g + 1) * N_CMP], src,
                                                colv("pe", kv * 16, kv * 16 + 16)[q].unsqueeze(2).to_broadcast([HD, 16, N_CMP]),
                                                ALU.add)
            ins.then_inc(cmp_blocks, 1)
            dve.wait_ge(vtok_sum, 1)
            dve.tensor_copy(v_tok.rearrange("p a b c -> p (a b c)"), psum[:, 4, :]).then_inc(vtok_ready, 1)
            dve.wait_ge(cmp_sum, 1)
            dve.tensor_copy(k_cmp[0:HD, :], psum[0:HD, 5, 0:N_CMP]).then_inc(cmp_ready, 1)
            dve.tensor_copy(k_cmp[HD:P, :], psum[HD:P, 5, N_CMP:2 * N_CMP]).then_inc(cmp_ready, 1)
            dve.tensor_copy(v_cmp[0:N_CMP, :], psum[0:N_CMP, 5, 64:64 + P]).then_inc(cmp_ready, 1)

            def short_conv():
                step(dve.tensor_tensor(conv_m, z1[:, ZC:ZC + 4, :], z1[:, ZX:ZX + 4, :], ALU.mult))
                for t in range(4):
                    ins = dve.tensor_scalar(mix[:, 4 + t, :], conv_m[:, t, :], colv("conv_mix", 3 * t + 2, 3 * t + 3),
                                            None, ALU.mult)
                step(ins)
                for back in (1, 2):
                    for t in range(4):
                        ins = dve.scalar_tensor_tensor(out=mix[:, 4 + t, back:TX], in0=conv_m[:, t, 0:TX - back],
                                                       scalar=colv("conv_mix", 3 * t + 2 - back, 3 * t + 3 - back),
                                                       in1=mix[:, 4 + t, back:TX], op0=ALU.mult, op1=ALU.add)
                    step(ins)
                dve.tensor_tensor(mix[:, 4:8, :], mix[:, 4:8, :], z1[:, ZB:ZB + 4, :], ALU.mult).then_inc(conv_ready, 1)

            def shift_max(z, bias, bank_ap, n):
                step(dve.scalar_tensor_tensor(out=z, in0=bank_ap, scalar=SCALE, in1=bias, op0=ALU.mult, op1=ALU.add))
                step(dve.tensor_reduce(red[:, 0, 0:REP], z, AX, ALU.max))
                dve.tensor_tensor(z, z, red[:, 0, 0:REP].unsqueeze(2).to_broadcast([P, REP, n]),
                                  ALU.subtract).then_inc(logits_ready, 1)

            def gated(z, branch, qt, g, n, mask=None):
                step(dve.tensor_reduce(red[:, 1, 0:REP], z, AX, ALU.add))
                step(dve.reciprocal(red[:, 1, 4:8], red[:, 1, 0:REP]))
                f = red[:, 1, 8:12]
                step(dve.tensor_tensor(f, red[:, 1, 4:8], gates[:, qt, branch * 8 + 4 * g:branch * 8 + 4 * g + 4], ALU.mult))
                if mask is not None:
                    step(dve.tensor_scalar(red[:, 1, 12:16], f, mask, None, ALU.mult))
                    f = red[:, 1, 12:16]
                dve.tensor_tensor(z, z, f.unsqueeze(2).to_broadcast([P, REP, n]), ALU.mult).then_inc(probs_ready, 1)

            dve.wait_ge(bias_ready, 6)
            dve.wait_ge(gates_ready, 1)
            turns = 0
            for gi in range(4):
                qt, g = gi // 2, gi % 2
                nk = P * (qt + 1)
                heads = slice(4 * g, 4 * g + 4)
                for b in range(2):
                    dve.wait_ge(logits_sum, 3 * gi + b + 1)
                    if gi > 0 and b == 0:
                        dve.wait_ge(turned, turns)
                    bank = psum[:, 2 * b:2 * b + 2, :].rearrange("p a (c k) -> p (a c) k", c=2)
                    shift_max(zbuf[:, b, :, 0:nk], bias_t[:, heads, TX - nk:TX], bank[:, :, 0:nk], nk)
                dve.wait_ge(logits_sum, 3 * gi + 3)
                shift_max(zbuf_c, bias_t[:, heads, 159 - qt * P:159 - qt * P + 16 * N_CMP - 15:16],
                          psum[:, 4, 0:64].rearrange("p (a b) -> p a b", a=REP)[:, :, 0:N_CMP], N_CMP)
                if gi == 0:
                    short_conv()
                for b in range(2):
                    dve.wait_ge(exps_ready, 3 * gi + b + 1)
                    gated(zbuf[:, b, :, 0:nk], 1 + b, qt, g, nk)
                dve.wait_ge(exps_ready, 3 * gi + 3)
                gated(zbuf_c, 0, qt, g, N_CMP, const("rowmask")[:, qt:qt + 1])
                turns += 2 * (qt + 1) + 1

            norm_post(1, y1, TX, 4, "mix_post")
            norm_pre(2, hx1, TX, 5, "ffn_pre")

            dve.sem_inc(ffn_conv_g, 2)
            dve.sem_inc(ffn_conv_u, 2)

            def ffn_dve(j, i=None):
                def trips(per, v):
                    return v if i is None else i * per + v

                par = j % 2
                at = COLS["ffn_conv"][0] + 6 * j
                src = col[:, at:at + 6] if i is None else col[:, bass.ds(i * 12 + at, 6)]
                dve.tensor_copy(taps[:, par, :], src).then_inc(ffn_taps, 1)
                dve.wait_ge(ffn_taps, trips(2, j + 1))
                for half, done in ((0, ffn_conv_g), (1, ffn_conv_u)):
                    dve.wait_ge(ffn_scaled, trips(4, 2 * j + half + 1))
                    c = ffn_c[:, par, half, :]
                    for back in (1, 2):
                        ins = dve.scalar_tensor_tensor(out=c[:, back:TX], in0=psum[:, 2 * par + half, 0:TX - back],
                                                       scalar=taps[:, par, 3 * half + 2 - back:3 * half + 3 - back],
                                                       in1=c[:, back:TX], op0=ALU.mult, op1=ALU.add)
                        if back == 1:
                            ins.then_inc(ffn_mid, 1)
                            dve.wait_ge(ffn_mid, trips(4, 2 * j + half + 1))
                        else:
                            ins.then_inc(done, 1)
                dve.wait_ge(ffn_gelu, trips(2, j + 1))
                dve.wait_ge(ffn_conv_u, trips(2, j + 3))
                dve.tensor_tensor(ffn_h[:, par, :], ffn_g[:, par, :], ffn_c[:, par, 1, :], ALU.mult).then_inc(ffn_hidden, 1)

            ffn_dve(0)
            with dve.Fori(0, (NF - 2) // 2) as i:
                ffn_dve(1, i)
                ffn_dve(2, i)
            ffn_dve(NF - 1)
            norm_post(3, y1, TX, 0, "ffn_post")

            norm_pre(4, hx, T2, 7, "mix2")
            zs = z2[:, :, 1:T2 + 1]

            dve.wait_ge(pads_zeroed, 2)
            dve.wait_ge(glu_sig, 1)
            step(dve.tensor_tensor(glu[:, :, TAPS - 1:], zs[:, 0:4], zs[:, 4:8], ALU.mult))
            for m in range(4):
                ins = dve.tensor_scalar(conv_y[:, m, :], glu[:, m, 0:T2], colv("conv_w", m * TAPS, m * TAPS + 1),
                                        colv("conv_b", m, m + 1), ALU.mult, ALU.add)
            for t in range(1, TAPS):
                for m in range(4):
                    if m % 2 == 0:
                        step(ins)
                    ins = dve.scalar_tensor_tensor(out=conv_y[:, m, :], in0=glu[:, m, t:t + T2],
                                                   scalar=colv("conv_w", m * TAPS + t, m * TAPS + t + 1),
                                                   in1=conv_y[:, m, :], op0=ALU.mult, op1=ALU.add)
            ins.then_inc(conv2_ready, 1)
            dve.wait_ge(cv_sum, 1)
            dve.tensor_scalar(rms[:, 1, :], psum[:, 6, 0:T2], 1.0 / 512, None, ALU.mult).then_inc(cv_mean, 1)
            dve.wait_ge(cv_mean, 1)
            dve.tensor_tensor(conv_y, conv_y, rms[:, 1, :].unsqueeze(1).to_broadcast([P, 4, T2]),
                              ALU.subtract).then_inc(cv_diff, 1)

            dve.wait_ge(in2_copied, RING + 22)
            step(dve.tensor_tensor(delta, z2[:, 8:22, 0:T2], zs[:, 8:22], ALU.subtract))
            for n in range(14):
                ins = dve.scalar_tensor_tensor(out=zs[:, 8 + n, :], in0=delta[:, n, :], scalar=colv("mu", n, n + 1),
                                               in1=zs[:, 8 + n, :], op0=ALU.mult, op1=ALU.add)
            ins.then_inc(shifted, 1)
            dve.wait_ge(cv_sum, 2)
            dve.tensor_scalar(rms[:, 0, :], psum[:, 6, 0:T2], 1.0 / 512, LN_EPS, ALU.mult, ALU.add).then_inc(cv_mean, 1)
            dve.wait_ge(cv_root, 1)
            step(dve.reciprocal(rms[:, 1, :], rms[:, 0, :]))
            dve.tensor_tensor(conv_y, conv_y, rms[:, 1, :].unsqueeze(1).to_broadcast([P, 4, T2]),
                              ALU.mult).then_inc(cv_scaled, 1)

            r_z, k_z, v_z = zs[:, 8:12], zs[:, 12:16], zs[:, 16:20]
            dve.wait_ge(shifted, 1)
            for m in range(4):
                ins = dve.tensor_scalar(kk[:, m, :], k_z[:, m, :], colv("k_k", m, m + 1), None, ALU.mult)
            ins.then_inc(kk_raw, 1)
            flat = lambda v: v.rearrange("p a b -> p (a b)")
            chunks = lambda v: v.rearrange("p a (c s) -> p (a c) s", s=CH)
            dve.wait_ge(up_ready, 4)
            step(dve.tensor_scalar(logdec, logdec, -float(np.exp(-0.5)), None, ALU.mult))
            step(dve.tensor_tensor_scan(flat(cum), const("scanmask"), flat(logdec), 0.0, ALU.mult, ALU.add))
            dve.tensor_tensor(e_prev, cum, logdec, ALU.subtract)
            dve.tensor_tensor(chunks(e_end), chunks(cum)[:, :, CH - 1:CH].to_broadcast([P, 4 * NCH, CH]), chunks(cum),
                              ALU.subtract).then_inc(cums_ready, 1)
            dve.wait_ge(kk_sum, 1)
            dve.tensor_scalar(k_new, psum[:, 4:8, 0:T2], 1e-24, None, ALU.max).then_inc(kk_mean, 1)
            dve.wait_ge(kk_root, 1)
            step(dve.reciprocal(b_vec, k_new))
            step(dve.tensor_tensor(kk, kk, b_vec, ALU.mult))
            dve.wait_ge(up_ready, 8)
            for m in range(4):
                ins = dve.tensor_scalar(k_new[:, m, :], a_gate[:, m, :], -1.0, colv("k_a", m, m + 1), ALU.add, ALU.mult)
            step(ins)
            dve.tensor_tensor(b_vec, kk, a_gate, ALU.mult)
            step(dve.scalar_tensor_tensor(out=k_new, in0=k_new, scalar=1.0, in1=k_z, op0=ALU.add, op1=ALU.mult))
            step(dve.tensor_tensor(sq4, r_z, k_new, ALU.mult))
            for m in range(4):
                ins = dve.tensor_scalar(sq4[:, m, :], sq4[:, m, :], colv("r_k", m, m + 1), None, ALU.mult)
            ins.then_inc(bonus_in, 1)
            dve.wait_ge(cexp_ready, 5)
            dve.tensor_tensor(alpha, kk, e_prev, ALU.mult)
            dve.scalar_tensor_tensor(out=beta, in0=b_vec, scalar=-1.0, in1=e_neg, op0=ALU.mult, op1=ALU.mult)
            dve.scalar_tensor_tensor(out=beta_end, in0=b_vec, scalar=-1.0, in1=e_end, op0=ALU.mult, op1=ALU.mult)
            dve.tensor_tensor(kappa, k_new, e_neg, ALU.mult)
            dve.tensor_tensor(kappa_end, k_new, e_end, ALU.mult)
            dve.tensor_tensor(rho, r_z, e_cum, ALU.mult).then_inc(feats_ready, 1)
            dve.wait_ge(bonus_sum, 1)
            dve.tensor_tensor(bonus, psum[:, 4:8, 0:T2], v_z, ALU.mult).then_inc(feats_ready, 1)

            for tg in range(3):
                t0, nt = tg * P, min(P, T2 - tg * P)
                for hh in range(2):
                    u = 2 * tg + hh
                    for n, (dst, kinds, mask) in enumerate(((G_LT, 2, "upper"), (G_L, 1, "lower"), (G_QT, 2, "upper_in"))):
                        for odd in range(2):
                            dve.wait_ge(gram_sum, 6 * u + 2 * n + odd + 1)
                            dve.tensor_tensor(gram[0:nt, dst:dst + kinds, odd::2, 0:nt],
                                              psum[0:nt, 2 * n + odd, 0:kinds * 2 * P].rearrange("p (k h t) -> p k h t", k=kinds, h=2)[:, :, :, 0:nt],
                                              const(mask)[0:nt, 0:nt].unsqueeze(1).unsqueeze(1).to_broadcast([nt, kinds, 2, nt]),
                                              ALU.mult).then_inc(gram_ready, 1)
                    for j in range(4):
                        dve.wait_ge(app_sum, 4 * u + j + 1)
                        if j > 0:
                            dve.wait_ge(app_ready, 4 * u + j)
                        dve.tensor_tensor(ycol[0:nt], by_head(psum[0:nt, j % 2, :]), ycol[0:nt],
                                          ALU.add).then_inc(app_ready, 1)
                    two = lambda v: v.rearrange("p (a b) -> p a b", a=4)[:, 0:2, 0:nt]
                    dve.wait_ge(eo_sum, u + 1)
                    dve.tensor_tensor(e_t[:, 2 * hh:2 * hh + 2, 0:nt], two(psum[:, 4, :]), rho[:, 2 * hh:2 * hh + 2, t0:t0 + nt],
                                      ALU.add).then_inc(eo_ready, 1)
                    dve.tensor_copy(o_in[:, 2 * hh:2 * hh + 2, 0:nt], two(psum[:, 5, :])).then_inc(eo_ready, 1)
                    if tg < 2:
                        for p in range(2):
                            n = 2 * u + p
                            if n > 0:
                                dve.wait_ge(fg_sum, n)
                            dve.wait_ge(app_ready, 4 * u + 4)
                            dve.tensor_tensor(expand[:, 2], ycol[:, 2 * p:2 * p + 2, HD:P].unsqueeze(2).to_broadcast([P, 2, 8, HD]),
                                              const("chunk").unsqueeze(1).unsqueeze(3).to_broadcast([P, 2, 8, HD]),
                                              ALU.mult).then_inc(spread_y, 1)
                            dve.wait_ge(fg_sum, n + 1)
                            dve.wait_ge(decay_diag, tg + 1)
                            ft = f_t[:, 2 * hh + p].rearrange("p a b -> p (a b)")
                            dve.tensor_tensor(ft, psum[:, 6, :], ft, ALU.add).then_inc(f_ready, 1)
                if tg < 2:
                    dve.wait_ge(g_ready, 4 * (tg + 1))
                    for c in range(8):
                        dve.wait_ge(rec_sum, 8 * tg + c + 1)
                        dve.tensor_tensor(state[:, :, c + 1, :], psum[:, c % 2, 0:4 * HD].rearrange("p (a b) -> p a b", a=4),
                                          g_c[:, :, c, :], ALU.add).then_inc(state_ready, 1)
                else:
                    dve.wait_ge(rec_sum, NCH)
                dve.wait_ge(eo_ready, 4 * (tg + 1))
                dve.tensor_tensor(o_all[:, :, t0:t0 + nt], by_head(psum[:, 2, :])[:, :, 0:nt], o_in[:, :, 0:nt],
                                  ALU.add).then_inc(o_ready, 1)

            dve.wait_ge(gn_sum, 1)
            dve.wait_ge(o_ready, 3)
            step(dve.scalar_tensor_tensor(out=gn_d, in0=psum[:, 0:4, 0:T2], scalar=-1.0 / HD, in1=o_all,
                                          op0=ALU.mult, op1=ALU.add))
            dve.tensor_tensor(gn_s, gn_d, gn_d, ALU.mult).then_inc(gn_sq, 1)
            dve.wait_ge(gn_sum, 2)
            dve.tensor_scalar(gn_s, psum[:, 4:8, 0:T2], 1.0 / HD, GN_EPS, ALU.mult, ALU.add).then_inc(gn_mean, 1)
            dve.wait_ge(gn_root, 1)
            step(dve.reciprocal(gn_s, gn_s))
            step(dve.tensor_tensor(gn_d, gn_d, gn_s, ALU.mult))
            for m in range(4):
                ins = dve.tensor_scalar(gn_d[:, m, :], gn_d[:, m, :], colv("gn_g", m, m + 1), colv("gn_b", m, m + 1),
                                        ALU.mult, ALU.add)
            step(ins)
            step(dve.tensor_tensor(gn_d, gn_d, bonus, ALU.add))
            dve.tensor_tensor(mid, gn_d[:, :, N_META:T2], gmul[:, :, N_META:T2], ALU.mult).then_inc(mid_ready, 1)

            for m in range(KD):
                b0 = 4 * (m % 2)
                dve.wait_ge(tiles_used, B_MID + 3 * m + 3)
                dve.wait_ge(gate_sig, m + 1)
                step(dve.tensor_tensor(part[:, m % 2], gate_s[:, m % 2], psum[:, b0 + 2:b0 + 4, 0:TX], ALU.mult))
                dve.tensor_tensor(merged[:, m, :], part[:, m % 2, 0, :], part[:, m % 2, 1, :], ALU.add).then_inc(merged_ready, 1)
            for m in range(KD):
                dve.wait_ge(tiles_used, B_OUT2 + m + 1)
                dve.tensor_tensor(hx1[:, m, :], psum[:, m, 0:TX], hx1[:, m, :], ALU.add).then_inc(out2_added, 1)
            dve.wait_ge(out2_added, KD)
            norm_pre(5, hx1, TX, 6, "ffn2")

            def sixteen(n, values, src, index):
                for j in range(n):
                    ins = dve.max(values[:, j, 0:8], src[:, j, :])
                step(ins)
                for j in range(n):
                    dve.max_index(index[:, j, 0:8], values[:, j, 0:8], src[:, j, :])
                    ins = dve.match_replace(src[:, j, :], values[:, j, 0:8], src[:, j, :], -3e38)
                step(ins)
                for j in range(n):
                    ins = dve.max(values[:, j, 8:16], src[:, j, :])
                step(ins)
                for j in range(n):
                    ins = dve.max_index(index[:, j, 8:16], values[:, j, 8:16], src[:, j, :])
                step(ins)

            dve.wait_ge(score_copied, 8)
            full = [P, 8, TOPK, TOPK]
            for qt in range(2):
                sixteen(16, best, score[:, qt], best_u)
                dve.tensor_copy(best_i, best_u)
                bh = best.rearrange("p (h c) k -> p h c k", c=2)
                step(dve.tensor_tensor(cand, bh[:, :, 0, :].unsqueeze(3).to_broadcast(full),
                                       bh[:, :, 1, :].unsqueeze(2).to_broadcast(full), ALU.add))
                sixteen(8, pick_s, cand.rearrange("p h a b -> p h (a b)"), pick_u)
                dve.tensor_single_scalar(pick_hi_u, pick_u, 4, ALU.logical_shift_right)
                step(dve.tensor_single_scalar(pick_lo_u, pick_u, 15, ALU.bitwise_and))
                dve.tensor_copy(pick_k[:, 0], pick_hi_u)
                dve.tensor_copy(pick_k[:, 1], pick_lo_u)
                step(dve.tensor_copy(soft[:, 0], pick_s[:, :, 0]))
                dve.tensor_tensor(pick_s, pick_s, soft[:, 0].unsqueeze(2).to_broadcast([P, 8, TOPK]),
                                  ALU.subtract).then_inc(pick_shift, 1)
                ih = best_i.rearrange("p (h c) k -> p h c k", c=2)
                for c in range(2):
                    step(dve.tensor_tensor(sel_eq, pick_k[:, c].unsqueeze(3).to_broadcast(full),
                                           const("iota")[:, 0:TOPK].unsqueeze(1).unsqueeze(1).to_broadcast(full), ALU.is_equal))
                    step(dve.tensor_tensor(sel_eq, sel_eq, ih[:, :, c, :].unsqueeze(2).to_broadcast(full), ALU.mult))
                    step(dve.tensor_reduce(chosen[:, 1 + c, qt], sel_eq, AX, ALU.add))
                dve.wait_ge(pick_exp, qt + 1)
                step(dve.tensor_reduce(soft[:, 0], pick_s, AX, ALU.add))
                step(dve.reciprocal(soft[:, 1], soft[:, 0]))
                dve.tensor_tensor(chosen[:, 0, qt], pick_s, soft[:, 1].unsqueeze(2).to_broadcast([P, 8, TOPK]),
                                  ALU.mult).then_inc(chosen_ready, 1)
                dve.wait_ge(chosen_ready, qt + 1)
            dve.wait_ge(chosen_sum, 1)
            for n in range(3):
                dve.tensor_copy(chosen_t[:, n, :], psum[:, n, 0:TX]).then_inc(chosen_turned, 1)
            dve.wait_ge(chosen_turned, 3)

            with dve.Fori(0, TX // 8) as i:
                for s in range(2):
                    dve.wait_ge(gates_copied, i * 2 + (s + 1))
                    for t in range(4):
                        ins = dve.tensor_scalar(hot[:, s, 0, t, :], const("iota"), chosen_t[:, 1, bass.ds(i * 8 + (4 * s + t), 1)],
                                                chosen_t[:, 0, bass.ds(i * 8 + (4 * s + t), 1)], ALU.is_equal, ALU.mult)
                    ins.then_inc(hot_a, 1)

            def expert(e, i=None):
                dve.wait_ge(expert_act, 3 + e + 1 if i is None else i * 3 + (3 + e + 1))
                g = gates_e[:, e, :] if i is None else gates_e[:, i * 3 + e, :]
                dve.tensor_tensor(coef_e[:, e % 3, :], act_e[:, e % 3, :], g, ALU.mult).then_inc(expert_coef, 1)

            expert(0)
            with dve.Fori(0, (NE - 1) // 3) as i:
                for s in range(1, 4):
                    expert(s, i)
            expert(NE - 1)
            dve.wait_ge(tiles_used, B_EXP + 2 * NE)
            for m in range(4):
                dve.tensor_tensor(hx1[:, 2 * m:2 * m + 2, :], psum[:, 4 + m, :].rearrange("p (a b) -> p a b", a=2),
                                  hx1[:, 2 * m:2 * m + 2, :], ALU.add).then_inc(out3_added, 1)
            dve.wait_ge(out3_added, 4)
            norm_pre(6, hx1, TX, 0, "final")


def kernel(**inputs):
    import numpy as np
    import concourse.bacc as bacc
    from concourse.bass_utils import run_bass_kernel_spmd

    a = {name: np.asarray(value) for name, value in inputs.items()}
    depth1 = {name: (v[0] if v.ndim > 1 and v.shape[0] == 1 else v) for name, v in a.items()}
    g = depth1

    def vec(v):
        return v.reshape(-1, P).T

    def taps(v):
        t, n = v.shape
        return v.reshape(t, n // P, P).transpose(2, 1, 0).reshape(P, -1)

    def tiles(w):
        k, n = w.shape
        return w.reshape(k // P, P, n // P, P).transpose(2, 1, 0, 3).reshape(n // P, P, -1)

    w = g["w_in"]
    heads = [w[:, h * HD:(h + 1) * HD] for i in range(REP) for h in (i, i + REP)]
    kv0 = N_HEADS * HD
    at = lambda n: w[:, kv0 + n * HD:kv0 + (n + 1) * HD]
    pairs = [at(n) for n in (0, 0, 1, 1, 2, 2, 3, 3)]
    gate0 = kv0 + 12 * HD
    w1_in = tiles(np.concatenate(heads + pairs + [w[:, kv0 + 4 * HD:gate0], w[:, gate0 + 24:]], 1))
    wg = w[:, gate0:gate0 + 24].reshape(KD, P, N_HEADS, 3).transpose(1, 0, 3, 2).reshape(P, KD * 24)

    def cmp_tiles(w1):
        return w1.reshape(2, 4, 4, HD, 2 * P).transpose(1, 0, 3, 2, 4).reshape(4, P, TW)

    w1_cmp = np.concatenate([cmp_tiles(g["w_cmp_k1"]), cmp_tiles(g["w_cmp_v1"])], 0)
    w_out = g["w_out"]
    order = [w_out[h * HD:(h + 1) * HD] for i in range(REP) for h in (i, i + REP)]
    w1_out = tiles(np.concatenate(order + [w_out[N_HEADS * HD:]], 0))
    up = tiles(g["w_ffn_up"]).reshape(2, NF, P, TW)
    dn = g["w_ffn_down"].reshape(NF, P, TW)
    w1_ffn = np.stack([t for j in range(NF + 1) for t in ([up[0, j], up[1, j]] if j < NF else [])
                       + ([dn[j - 1]] if j else [])], 0)
    fc = g["ffn_conv_w"].reshape(3, 2, NF, P).transpose(3, 2, 1, 0).reshape(P, -1)
    pe = np.concatenate([g[n].reshape(2, 16, HD).transpose(0, 2, 1).reshape(P, 16) for n in ("pe_cmp_k", "pe_cmp_v")], 1)
    w2k = g["w_cmp_k2"].reshape(2, P, HD)
    w2k = np.concatenate([w2k, w2k], 2).transpose(1, 0, 2).reshape(P, 2 * P)
    w2v = g["w_cmp_v2"].reshape(2, P, HD).transpose(1, 0, 2).reshape(P, P)

    columns = {
        "mix_pre": vec(g["norm_mix_pre"]), "mix_post": vec(g["norm_mix_post"]), "ffn_pre": vec(g["norm_ffn_pre"]),
        "ffn_post": vec(g["norm_ffn_post"]), "mix2": vec(g["g_mix_2"]), "ffn2": vec(g["g_ffn_2"]),
        "final": vec(g["g_final_2"]), "conv_mix": taps(g["conv_mix_w"]), "ffn_conv": fc, "pe": pe, "gates": wg,
        "w2k": w2k, "w2v": w2v, "conv_w": taps(g["conv_w_2"]), "conv_b": vec(g["conv_b_2"]),
        "ln_g": vec(g["conv_ln_g_2"]), "ln_b": vec(g["conv_ln_b_2"]), "mu": vec(g["mu_shift_2"]), "w0": vec(g["w0_2"]),
        "a0": vec(g["a0_2"]), "k_k": vec(g["k_k_2"]), "k_a": vec(g["k_a_2"]), "r_k": vec(g["r_k_2"].reshape(-1)),
        "gn_g": vec(g["gn_g_2"]), "gn_b": vec(g["gn_b_2"]),
        "wa_up": np.concatenate([g["w_up_2"], g["a_up_2"]], 0), "g_up": g["g_up_2"],
    }
    cols = np.concatenate([columns[name] for name in COLS], 1)

    w2 = tiles(g["w_in_2"])
    w2_in = w2[:22]
    branches = tiles(np.concatenate([g["w_conv_out_2"], g["w_rwkv_out_2"]], 0))
    w2_mid = np.stack([t for m in range(KD) for t in (w2[22 + m], w2[30 + m], branches[m])], 0)
    w2_out = tiles(g["w_o_2"])
    w2_q = tiles(g["w_q_2"])
    w2_sub = g["sub_keys_2"].reshape(2, 8, NE, P).transpose(0, 3, 1, 2).reshape(2, P, TW)
    eu = g["expert_u_2"].reshape(NE, NE, KD, P)
    ev = g["expert_v_2"].reshape(NE, NE, TW)
    experts = np.empty((2 * NE, P, TW), np.float32)
    u_at = [0] + [2 * e - 1 for e in range(1, NE)]
    v_at = [2 * e + 2 for e in range(NE - 1)] + [2 * NE - 1]
    for e in range(NE):
        experts[u_at[e]] = eu[:, e].transpose(2, 1, 0).reshape(P, TW)
        experts[v_at[e]] = ev[:, e]

    arrays = {
        "x_t": a["x"].reshape(TX, KD, P).transpose(2, 1, 0), "meta_t": g["meta_tokens_2"].reshape(N_META, KD, P).transpose(2, 1, 0),
        "cols": cols, "consts": shape_constants(), "rel": a["rel_bias"].T, "w1_in": w1_in, "w1_cmp": w1_cmp,
        "w1_out": w1_out, "w1_ffn": w1_ffn, "w2_in": w2_in, "w2_mid": w2_mid, "w2_out": w2_out, "w2_q": w2_q,
        "w2_sub": w2_sub, "experts": experts,
    }
    arrays = {name: np.ascontiguousarray(v) for name, v in arrays.items()}
    nc = bacc.Bacc("TRN2", target_bir_lowering=False, num_devices=1)
    ins = [nc.dram_tensor(name, v.shape, F32, kind="ExternalInput").ap() for name, v in arrays.items()]
    out = nc.dram_tensor("out_t", (P, KD, TX), F32, kind="ExternalOutput").ap()
    rows = nc.dram_tensor("bias_rows", (N_HEADS, 512), F32, kind="Internal").ap()
    bass_transformer_pair(nc, *ins, out, rows)
    got = run_bass_kernel_spmd(nc, [arrays], core_ids=[0]).results[0]["out_t"]
    return got.transpose(2, 1, 0).reshape(1, TX, D)
```

```python
import numpy as np
import concourse.bass as bass
import concourse.mybir as mybir
from contextlib import ExitStack

P = 128
D = 1024
KD = D // P
TX = 256
N_META = 16
T2 = TX + N_META
TW = KD * P
RING = 3
BODY = 6

HD = 64
N_HEADS = 8
N_KV = 2
REP = N_HEADS // N_KV
N_CMP = (TX - 32) // 16 + 1
D_FF = 2816
NF = D_FF // P
NEG = -1e30
EPS = 1e-6
SCALE = HD ** -0.5
Z1 = 24
ZQ, ZKC, ZVC, ZKS, ZVS, ZKW, ZVW, ZB, ZC, ZX = 0, 4, 6, 8, 9, 10, 11, 12, 16, 20

Z2 = 38
NCH = T2 // 16
CH = 16
LN_EPS = 1e-5
GN_EPS = 64e-5
TAPS = 31
NE = 128
TOPK = 16

F32 = mybir.dt.float32
F32R = mybir.dt.float32r
U32 = mybir.dt.uint32
ALU = mybir.AluOpType
ACT = mybir.ActivationFunctionType
AX = mybir.AxisListType.X


def layout(parts):
    at, n = {}, 0
    for name, width in parts:
        at[name] = (n, width)
        n += width
    return at, n


KEPT, N_KEPT = layout([
    ("ident", P), ("ones", P), ("headones", P), ("identhead", HD), ("lower", P), ("upper", P), ("upper_in", P),
    ("chunk", 8), ("rowmask", 2), ("iota", P),
    ("mix_pre", 8), ("mix_post", 8), ("ffn_pre", 8), ("ffn_post", 8), ("mix2", 8), ("ffn2", 8), ("final", 8),
    ("conv_mix", 12), ("conv_b", 4), ("ln_g", 4), ("ln_b", 4), ("mu", 14), ("w0", 4), ("a0", 4), ("k_k", 4),
    ("k_a", 4), ("r_k", 4), ("gn_g", 4), ("gn_b", 4)])
FIRST, N_FIRST = layout([("ffn_conv", 3 * 2 * NF), ("pe", 32), ("gates", KD * 24), ("w2k", 256), ("w2v", 128),
                         ("onehot", 512), ("flip", P)])
SECOND, N_SECOND = layout([("conv_w", 4 * TAPS), ("wa_up", 512), ("g_up", 512), ("scanmask", T2)])


def shape_constants():
    c = {}

    def put(name, value):
        c[name] = np.zeros((P, value.shape[1]), np.float32)
        c[name][:value.shape[0]] = value

    i = np.arange(P)
    same = i[:, None] // CH == i[None, :] // CH
    put("ident", np.eye(P))
    put("ones", np.ones((P, P)))
    put("flip", np.eye(P)[::-1])
    put("headones", (i[:, None] // HD == i[None, :] // HD) * 1.0)
    put("identhead", (i[:, None] % HD == np.arange(HD)[None, :]) * 1.0)
    put("lower", (same & (i[:, None] > i[None, :])) * 1.0)
    put("upper", (same & (i[:, None] < i[None, :])) * 1.0)
    put("upper_in", (same & (i[:, None] <= i[None, :])) * 1.0)
    put("chunk", (i[:, None] // CH == np.arange(8)[None, :]) * 1.0)
    put("rowmask", np.stack([i >= 31, i >= 0], 1) * 1.0)
    dist = 255 - np.arange(512)
    far = 16 + (np.log(np.maximum(dist, 1).astype(np.float32) / np.float32(16))
                / np.float32(np.log(128 / 16)) * np.float32(16)).astype(np.int32)
    bucket = np.where(dist < 16, dist, np.minimum(far, 31))
    bucket = np.where(dist < 0, 32, bucket)
    put("onehot", (np.arange(33)[:, None] == bucket[None, :]) * 1.0)
    put("iota", np.broadcast_to(i, (P, P)) * 1.0)
    put("scanmask", np.broadcast_to((np.arange(T2) % CH != 0), (P, T2)) * 1.0)
    return c


def bass_transformer_pair(nc, x_t, meta_t, kept, first, second, rel, w1_in, w1_cmp, w1_out, w1_ffn,
                          w2_in, w2_mid, w2_out, w2_q, w2_sub, experts, out_t, bias_rows):
    with ExitStack() as ctx:
        def sb(name, shape, dt=F32):
            return ctx.enter_context(nc.sbuf_tensor(name, shape, dt))

        def sem(name):
            return ctx.enter_context(nc.semaphore(name))

        ring = sb("ring", [P, RING, TW])
        w_hi = sb("w_hi", [P, RING, TW], F32R)
        w_lo = sb("w_lo", [P, RING, TW], F32R)
        kept_sb = sb("kept_sb", [P, N_KEPT])
        hx = sb("hx", [P, KD, T2])
        x_hi = sb("x_hi", [P, KD, T2], F32R)
        x_lo = sb("x_lo", [P, KD, T2], F32R)
        h_hi = sb("h_hi", [P, 2, TX], F32R)
        h_lo = sb("h_lo", [P, 2, TX], F32R)
        sq = sb("sq", [P, KD, T2])
        rms = sb("rms", [P, T2])
        zeros = sb("zeros", [P, P])
        big = sb("big", [P, NE * TX])
        psum = ctx.enter_context(nc.psum_tensor("psum", [P, 8, 512], F32))

        def carve(at, *dims):
            n = int(np.prod(dims))
            v = big[:, at:at + n]
            if len(dims) == 2:
                v = v.rearrange("p (a b) -> p a b", a=dims[0])
            if len(dims) == 3:
                v = v.rearrange("p (a b c) -> p a b c", a=dims[0], b=dims[1])
            if len(dims) == 4:
                v = v.rearrange("p (a b c d) -> p a b c d", a=dims[0], b=dims[1], c=dims[2])
            return v

        hx1 = hx[:, :, N_META:T2]
        first_sb = carve(NE * TX - N_SECOND - N_FIRST, N_FIRST)
        second_sb = carve(NE * TX - N_SECOND, N_SECOND)

        def colv(name, a=0, b=None):
            for part, sbuf in ((KEPT, kept_sb[:]), (FIRST, first_sb), (SECOND, second_sb)):
                if name in part:
                    o, w = part[name]
                    return sbuf[:, o + a:o + (w if b is None else b)]

        const = colv
        at = [0]

        def room(*dims):
            v = carve(at[0], *dims)
            at[0] += int(np.prod(dims))
            return v

        z1 = room(Z1, TX)
        bias_t = room(N_HEADS, 3 * P)
        cmp_in = room(2, 16, 2 * N_CMP)
        cmp_hid = room(2, 2, 2 * N_CMP)
        v_tok = room(2, 2, P)
        k_cmp = room(N_CMP)
        v_cmp = room(P)
        gates = room(2, 24)
        zbuf = room(2, REP, TX)
        zbuf_c = room(REP, N_CMP)
        red = room(2, 16)
        probs_t = room(2, 5, REP * P)
        mix_y = big[:, at[0]:at[0] + 2 * KD * TX]
        mix = room(KD, TX)
        y1 = room(KD, TX)
        bias_up = mix_y[:, 0:N_HEADS * 3 * P].rearrange("p (h k) -> p h k", h=N_HEADS)
        conv_m = room(4, TX)
        oh_tab = room(8)
        brow = room(512)
        ffn_c = room(2, 2, TX)
        ffn_g = room(2, TX)
        ffn_h = room(2, TX)
        taps = room(2, 6)
        assert at[0] <= NE * TX - N_SECOND - N_FIRST

        param_loaded = sem("param_loaded")
        x_loaded = sem("x_loaded")
        first_loaded = sem("first_loaded")
        second_loaded = sem("second_loaded")
        rel_loaded = sem("rel_loaded")
        high_ready = sem("high_ready")
        low_ready = sem("low_ready")
        norm_part = sem("norm_part")
        high_part = sem("high_part")
        x_split = sem("x_split")
        tile_landed = [sem(f"tile_landed{s}") for s in range(RING)]
        hidden_high = sem("hidden_high")
        hidden_low = sem("hidden_low")
        ffn_whole = sem("ffn_whole")
        coef_high = sem("coef_high")
        coef_low = sem("coef_low")
        tiles_used = sem("tiles_used")
        dve_step = sem("dve_step")
        act_step = sem("act_step")
        norm_squares = sem("norm_squares")
        norm_sums = sem("norm_sums")
        norm_mean = sem("norm_mean")
        norm_root = sem("norm_root")
        norm_out = sem("norm_out")
        in1_even = sem("in1_even")
        in1_odd = sem("in1_odd")
        gates_sum = sem("gates_sum")
        gates_ready = sem("gates_ready")
        neg_row = sem("neg_row")
        brow_sum = sem("brow_sum")
        brow_ready = sem("brow_ready")
        brow_stored = sem("brow_stored")
        bias_loaded = sem("bias_loaded")
        bias_turned = sem("bias_turned")
        bias_ready = sem("bias_ready")
        BIAS_BANKS = (0, 1, 2, 3, 6, 7)
        vtok_sum = sem("vtok_sum")
        vtok_ready = sem("vtok_ready")
        cmp_blocks = sem("cmp_blocks")
        cmp_hid_sum = sem("cmp_hid_sum")
        cmp_hid_ready = sem("cmp_hid_ready")
        cmp_sum = sem("cmp_sum")
        cmp_ready = sem("cmp_ready")
        logits_sum = sem("logits_sum")
        logits_ready = sem("logits_ready")
        exps_ready = sem("exps_ready")
        probs_ready = sem("probs_ready")
        turned = sem("turned")
        turned_copied = sem("turned_copied")
        heads_sum = sem("heads_sum")
        heads_ready = sem("heads_ready")
        conv_ready = sem("conv_ready")
        out1_ready = sem("out1_ready")
        zeros_ready = sem("zeros_ready")
        ffn_mid = sem("ffn_mid")
        ffn_scaled = sem("ffn_scaled")
        ffn_conv_g = sem("ffn_conv_g")
        ffn_conv_u = sem("ffn_conv_u")
        ffn_gelu = sem("ffn_gelu")
        ffn_taps = sem("ffn_taps")
        ffn_copied = sem("ffn_copied")
        out_stored = sem("out_stored")
        at[0] = 0
        z2 = room(22, T2 + 1)
        alpha = room(4, T2)
        beta = room(4, T2)
        kappa = room(4, T2)
        rho = room(4, T2)
        beta_end = room(4, T2)
        kappa_end = room(4, T2)
        bonus = room(4, T2)
        gmul = room(4, T2)
        glu = room(4, T2 + TAPS - 1)
        conv_y = room(4, T2)
        chunk_decay = room(4, NCH)
        tm = room(4, 4 * P)
        scratch0 = at[0]
        gram = room(10, 4, P)
        ycol = room(4, P)
        f_t = room(4, 8, HD)
        g_c = room(4, 8, HD)
        state = room(4, 9, HD)
        top1 = at[0]
        expand = carve(scratch0, 3, 2, 8, HD)
        G_L, G_LT, G_MT, G_L2, G_L2T, G_L4, G_L4T, G_L8T, G_QT, G_RT = range(10)
        at[0] = scratch0
        delta = room(14, T2)
        at[0] = scratch0
        logdec = room(4, T2)
        cum = room(4, T2)
        a_gate = room(4, T2)
        kk = room(4, T2)
        k_new = room(4, T2)
        b_vec = room(4, T2)
        e_cum = room(4, T2)
        e_prev = room(4, T2)
        e_neg = room(4, T2)
        e_end = room(4, T2)
        assert max(at[0], top1) <= NE * TX - N_SECOND
        sqf = sq[:, :, :].rearrange("p a b -> p (a b)")
        sq4 = sqf[:, 0:4 * T2].rearrange("p (a b) -> p a b", a=4)
        e_t = sqf[:, 0:4 * P].rearrange("p (a b) -> p a b", a=4)
        o_in = sqf[:, 4 * P:8 * P].rearrange("p (a b) -> p a b", a=4)
        o_all = sqf[:, 8 * P:8 * P + 4 * T2].rearrange("p (a b) -> p a b", a=4)
        at[0] = scratch0
        gn_d = room(4, T2)
        gn_s = room(4, T2)
        mid = room(4, TX)
        merged = room(8, TX)
        gate_z = z2[:, 0:16, 1:TX + 1]
        part = room(2, 2, TX)
        at[0] = 0
        query = room(16, TX)
        at[0] = NE * TX - 7696
        score = room(2, 16, NE)
        best = room(16, TOPK)
        best_i = room(16, TOPK)
        best_u = room(16, TOPK).bitcast(U32)
        cand = room(8, TOPK, TOPK)
        pick_k = room(2, 8, TOPK)
        pick_s = room(8, TOPK)
        pick_u = room(8, TOPK).bitcast(U32)
        pick_hi_u = room(8, TOPK).bitcast(U32)
        pick_lo_u = room(8, TOPK).bitcast(U32)
        sel_eq = cand
        soft = room(2, 8)
        FREE_EXPERTS = (NE * TX - 7696) // TX
        assert at[0] <= NE * TX and 16 * TX <= NE * TX - 7696
        chosen = sqf[:, 0:6 * P].rearrange("p (n q h k) -> p n q h k", n=3, q=2, h=8)
        chosen_t = sqf[:, 8 * P:8 * P + 4 * TX].rearrange("p (n t) -> p n t", n=4)
        hot_1 = sqf[:, 0:8 * P].rearrange("p (s t n) -> p s t n", s=2, t=4)
        hot_2 = x_hi[:].rearrange("p a b -> p (a b)")[:, 0:8 * P].rearrange("p (s t n) -> p s t n", s=2, t=4)
        off_1 = x_lo[:].rearrange("p a b -> p (a b)")[:, 0:8 * P].rearrange("p (s t n) -> p s t n", s=2, t=4)
        act_all = big[:, :].rearrange("p (e t) -> p e t", e=NE)

        meta_loaded = sem("meta_loaded")
        pads_zeroed = sem("pads_zeroed")
        in2_copied = sem("in2_copied")
        glu_sig = sem("glu_sig")
        conv2_ready = sem("conv2_ready")
        shifted = sem("shifted")
        lowrank_ready = sem("lowrank_ready")
        up_sum = sem("up_sum")
        up_ready = sem("up_ready")
        kk_raw = sem("kk_raw")
        kk_squares = sem("kk_squares")
        kk_sum = sem("kk_sum")
        kk_mean = sem("kk_mean")
        kk_root = sem("kk_root")
        cums_ready = sem("cums_ready")
        cexp_ready = sem("cexp_ready")
        feats_ready = sem("feats_ready")
        bonus_in = sem("bonus_in")
        bonus_sum = sem("bonus_sum")
        tm_sum = sem("tm_sum")
        tm_ready = sem("tm_ready")
        gram_sum = sem("gram_sum")
        gram_ready = sem("gram_ready")
        mv_sum = sem("mv_sum")
        y_ready = sem("y_ready")
        pow_sum = sem("pow_sum")
        pow_ready = sem("pow_ready")
        app_sum = sem("app_sum")
        app_ready = sem("app_ready")
        eo_sum = sem("eo_sum")
        eo_ready = sem("eo_ready")
        spread_b = sem("spread_b")
        decay_diag = sem("decay_diag")
        fg_sum = sem("fg_sum")
        f_ready = sem("f_ready")
        g_ready = sem("g_ready")
        rec_sum = sem("rec_sum")
        state_ready = sem("state_ready")
        o_ready = sem("o_ready")
        cv_sum = sem("cv_sum")
        cv_mean = sem("cv_mean")
        cv_root = sem("cv_root")
        cv_out = sem("cv_out")
        gn_sum = sem("gn_sum")
        gn_sq = sem("gn_sq")
        gn_mean = sem("gn_mean")
        gn_root = sem("gn_root")
        mid_ready = sem("mid_ready")
        gate_sig = sem("gate_sig")
        merged_ready = sem("merged_ready")
        out2_added = sem("out2_added")
        q_copied = sem("q_copied")
        score_copied = sem("score_copied")
        pick_shift = sem("pick_shift")
        pick_exp = sem("pick_exp")
        chosen_ready = sem("chosen_ready")
        chosen_sum = sem("chosen_sum")
        chosen_turned = sem("chosen_turned")
        hot_a = sem("hot_a")
        hot_b = sem("hot_b")
        gates_done = sem("gates_done")
        gates_used = sem("gates_used")
        expert_act = sem("expert_act")
        off_ready = sem("off_ready")
        cv_squares = sem("cv_squares")
        cv_diff = sem("cv_diff")
        spread_y = sem("spread_y")
        score_sum = sem("score_sum")
        out3_added = sem("out3_added")
        cv_scaled = sem("cv_scaled")

        def by_head(bank):
            return bank.rearrange("p (h t) -> p h t", h=4)


        stream = [(w1_in, Z1), (w1_cmp, 8), (w1_out, KD), (w1_ffn, 3 * NF)]
        stream += [(w2_in, 22), (w2_mid, 3 * KD), (w2_out, KD), (w2_q, 16), (w2_sub, 2), (experts, 2 * NE)]
        base, n = [], 0
        for _, count in stream:
            base.append(n)
            n += count
        B_IN1, B_CMP, B_OUT1, B_FFN = base[:4]
        B_IN2, B_MID, B_OUT2, B_Q, B_SUB, B_EXP = base[4:]

        def trip(v, i=None, per=BODY):
            return v if i is None else i * per + v

        N_TILES = B_EXP + 2 * NE
        AHEAD = RING - 1

        def split_high(act, n, i=None):
            act.wait_ge(tile_landed[n % RING], trip(16 * (n // RING + 1), i, 16 * BODY // RING))
            if n >= RING:
                act.wait_ge(tiles_used, trip(n - RING + 1, i))
            act.activation(w_hi[:, n % RING, :], ring[:, n % RING, :], ACT.Copy).then_inc(high_ready, 1)

        def split_low(dve, n, i=None):
            dve.wait_ge(high_ready, trip(n + 1, i))
            dve.tensor_tensor(w_lo[:, n % RING, :], ring[:, n % RING, :], w_hi[:, n % RING, :].bitcast(F32),
                              ALU.subtract).then_inc(low_ready, 1)

        def tile_split(pe, n, i=None):
            pe.wait_ge(low_ready, trip(n + 1, i))
            return n % RING

        X_NORM0, X_MIX, X_NORM2, X_NORM4, X_BRANCH, X_MERGED, X_NORM5 = range(7)
        B_V = B_EXP + NE
        branch_in = lambda q: conv_y[:, 2 * q:2 * q + 2, N_META:T2] if q < 2 else mid[:, 2 * q - 4:2 * q - 2, :]

        def pieces(b, count, eng, body):
            trips = count // BODY
            if trips > 1:
                with eng.Fori(0, trips) as i:
                    for k in range(BODY):
                        body(k, i)
            for k in range(trips * BODY if trips > 1 else 0, count):
                body(k, None)

        block = ctx.enter_context(nc.Block())

        @block.sync
        def _(sp):
            sp.dma_start(hx1, x_t).then_inc(x_loaded, 16)
            sp.dma_start(hx[:, :, 0:N_META], meta_t).then_inc(meta_loaded, 16)
            sp.dma_start(kept_sb[:], kept).then_inc(param_loaded, 16)
            sp.dma_start(first_sb, first).then_inc(first_loaded, 16)
            sp.dma_start(oh_tab[0:32, :], rel).then_inc(rel_loaded, 16)

            def load_tile(src, n, t, free):
                if free is not None:
                    sp.wait_ge(low_ready, free)
                sp.dma_start(ring[:, n % RING, :], src[t]).then_inc(tile_landed[n % RING], 16)

            for (src, count), b in zip(stream, base):
                t0 = 0
                if b == 0:
                    for t in range(BODY):
                        load_tile(src, t, t, t - RING + 1 if t >= RING else None)
                    sp.dma_start(second_sb, second).then_inc(second_loaded, 16)
                    t0 = BODY
                trips = (count - t0) // BODY
                if trips > 1:
                    with sp.Fori(0, trips) as i:
                        for k in range(BODY):
                            load_tile(src, b + t0 + k, i * BODY + (t0 + k), i * BODY + (b + t0 + k - RING + 1))
                    t0 += trips * BODY
                for t in range(t0, count):
                    load_tile(src, b + t, t, b + t - RING + 1)

            sp.wait_ge(norm_out, 3)
            sp.dma_start(out_t, sq[:, :, 0:TX]).then_inc(out_stored, 16)
            sp.wait_ge(out_stored, 16)

        @block.gpsimd
        def _(pool):
            pool.memset(zeros[:], 0.0).then_inc(zeros_ready, 1)
            pool.wait_ge(zeros_ready, 1)
            pool.memset(oh_tab[32:33, :], NEG).then_inc(neg_row, 1)
            pool.wait_ge(brow_ready, 1)
            pool.dma_start(bias_rows, brow[0:N_HEADS, :]).then_inc(brow_stored, 16)
            pool.wait_ge(brow_stored, 16)
            rows = bias_rows.tensor

            pool.dma_start(bias_up, bass.AP(tensor=rows, offset=0, ap=[[1, P], [512, N_HEADS], [1, 3 * P]])).then_inc(bias_loaded, 16)

            pool.wait_ge(norm_out, 2)
            pool.memset(z2[:, :, 0:1], 0.0).then_inc(pads_zeroed, 1)
            pool.memset(glu[:, :, 0:TAPS - 1], 0.0).then_inc(pads_zeroed, 1)
            pool.wait_ge(feats_ready, 2)
            pool.wait_ge(cexp_ready, 5)
            pool.memset(state[:, :, 0, :], 0.0).then_inc(state_ready, 1)
            for tg in range(2):
                if tg > 0:
                    pool.wait_ge(o_ready, tg)
                pool.tensor_tensor(f_t, const("identhead").unsqueeze(1).unsqueeze(1).to_broadcast([P, 4, 8, HD]),
                                   chunk_decay[:, :, 8 * tg:8 * tg + 8].unsqueeze(3).to_broadcast([P, 4, 8, HD]),
                                   ALU.mult).then_inc(decay_diag, 1)
                for hh in range(2):
                    for p in range(2):
                        n = 4 * tg + 2 * hh + p
                        pool.wait_ge(app_ready, 4 * (2 * tg + hh + 1))
                        if n > 0:
                            pool.wait_ge(fg_sum, n)
                        for k, src in ((0, 3), (1, 1)):
                            a = (4 * hh + 2 * p) * HD
                            pool.tensor_tensor(expand[:, k], tm[:, src, a:a + P].rearrange("p (h k) -> p h k", h=2).unsqueeze(2).to_broadcast([P, 2, 8, HD]),
                                               const("chunk").unsqueeze(1).unsqueeze(3).to_broadcast([P, 2, 8, HD]),
                                               ALU.mult).then_inc(spread_b, 1)

        @block.tensor
        def _(pe):
            def norm_pe(n, width, bank):
                pe.wait_ge(norm_squares, n + 1)
                for k in range(KD):
                    mm = pe.matmul(psum[:, bank, 0:width], const("ones"), sq[:, k, 0:width],
                                   start=(k == 0), stop=(k == KD - 1))
                mm.then_inc(norm_sums, 1)

            def project(slot, dst, width, chunks=range(KD), t0=0):
                n = 0
                for k in chunks:
                    for w, x in ((w_hi, x_hi), (w_hi, x_lo), (w_lo, x_hi)):
                        mm = pe.matmul(dst, w[:, slot, k * P:(k + 1) * P], x[:, k, t0:t0 + width],
                                       start=(n == 0), stop=(n == 3 * len(chunks) - 1))
                        n += 1
                return mm

            def zero_y():
                for m in range(4):
                    pe.matmul(psum[:, 4 + m, :], zeros[:], kept_sb[:, 0:512], start=True, stop=False, skip_group_check=True)

            def down(slot, par):
                for m in range(KD):
                    for w, h in ((w_hi, h_hi), (w_hi, h_lo), (w_lo, h_hi)):
                        mm = pe.matmul(psum[:, 4 + m // 2, (m % 2) * TX:(m % 2 + 1) * TX], w[:, slot, m * P:(m + 1) * P],
                                       h[:, par, :], start=False, stop=False, skip_group_check=True)
                return mm

            pe.wait_ge(param_loaded, 16)
            pe.wait_ge(first_loaded, 16)
            pe.wait_ge(rel_loaded, 16)
            pe.wait_ge(neg_row, 1)
            pe.matmul(psum[0:N_HEADS, 7, :], oh_tab[0:33, :], const("onehot")[0:33, :],
                      start=True, stop=True).then_inc(brow_sum, 1)

            norm_pe(0, TX, 6)
            pe.wait_ge(x_split, X_NORM0 + 1)
            for qt in range(2):
                for k in range(KD):
                    mm = pe.matmul(psum[:, 6, qt * 24:(qt + 1) * 24], sq[:, k, qt * P:(qt + 1) * P],
                                   colv("gates", k * 24, (k + 1) * 24), start=(k == 0), stop=(k == KD - 1))
            mm.then_inc(gates_sum, 1)
            with pe.Fori(0, Z1 // BODY) as i:
                for k in range(BODY):
                    slot = tile_split(pe, B_IN1 + k, i)
                    pe.wait_ge((in1_even, in1_odd)[k % 2], i * 3 + (k // 2 + 1))
                    project(slot, psum[:, k, 0:TX], TX).then_inc(tiles_used, 1)

            for kv in range(2):
                pe.wait_ge(cmp_blocks, 1)
                for j in range(4):
                    slot = tile_split(pe, B_CMP + kv * 4 + j)
                    for r in range(4):
                        for c in range(2):
                            for n, w in enumerate((w_hi, w_lo)):
                                mm = pe.matmul(psum[:, 2 * kv + c, 0:2 * N_CMP], w[:, slot, (r * 2 + c) * P:(r * 2 + c + 1) * P].bitcast(F32),
                                               cmp_in[:, kv, 4 * j + r, :], start=(j + r + n == 0), stop=(j + r + n == 7))
                    mm.then_inc(tiles_used, 1)
            for b, zt in enumerate((ZVS, ZVW)):
                for kt in range(2):
                    mm = pe.transpose(psum[:, 4, (b * 2 + kt) * P:(b * 2 + kt + 1) * P],
                                      z1[:, zt, kt * P:(kt + 1) * P], const("ident"))
            mm.then_inc(vtok_sum, 1)
            pe.wait_ge(cmp_hid_ready, 4)
            for c in range(2):
                pe.matmul(psum[:, 5, 0:2 * N_CMP], colv("w2k", c * P, (c + 1) * P), cmp_hid[:, 0, c, :],
                          start=(c == 0), stop=(c == 1))
            for g in range(N_KV):
                for c in range(2):
                    mm = pe.matmul(psum[0:N_CMP, 5, 64 + g * HD:64 + (g + 1) * HD],
                                   cmp_hid[:, 1, c, g * N_CMP:(g + 1) * N_CMP], colv("w2v", c * HD, (c + 1) * HD),
                                   start=(c == 0), stop=(c == 1))
            mm.then_inc(cmp_sum, 1)

            pe.wait_ge(bias_loaded, 16)
            pe.wait_ge(gates_ready, 1)
            pe.wait_ge(brow_ready, 1)
            for n in range(6):
                pe.matmul(psum[:, BIAS_BANKS[n], :], const("flip"), mix_y[:, n * 512:(n + 1) * 512],
                          start=True, stop=True).then_inc(bias_turned, 1)

            batches = [0]

            def logits(gi):
                qt, g = gi // 2, gi % 2
                half = slice(g * HD, (g + 1) * HD)
                nk = P * (qt + 1)
                for b, kt in enumerate((ZKS, ZKW)):
                    if gi > 0:
                        pe.wait_ge(logits_ready, 3 * (gi - 1) + b + 1)
                    for i in range(REP):
                        mm = pe.matmul(psum[:, 2 * b + i // 2, (i % 2) * TX:(i % 2) * TX + nk],
                                       z1[half, ZQ + i, qt * P:(qt + 1) * P], z1[half, kt, 0:nk], start=True, stop=True)
                    mm.then_inc(logits_sum, 1)
                if gi == 0:
                    pe.wait_ge(cmp_ready, 3)
                    pe.wait_ge(vtok_ready, 1)
                else:
                    pe.wait_ge(logits_ready, 3 * gi)
                for i in range(REP):
                    mm = pe.matmul(psum[:, 4, i * 16:i * 16 + N_CMP], z1[half, ZQ + i, qt * P:(qt + 1) * P],
                                   k_cmp[half, :], start=True, stop=True)
                mm.then_inc(logits_sum, 1)

            def turn(gi, b, src, rows):
                bank = 5 + batches[0] % 2
                if batches[0] >= 2:
                    pe.wait_ge(turned_copied, batches[0] - 1)
                for i in range(REP):
                    mm = pe.transpose(psum[0:rows, bank, i * P:(i + 1) * P], src(i), const("ident"))
                mm.then_inc(turned, 1)
                batches[0] += 1

            def attend(gi):
                qt, g = gi // 2, gi % 2
                for b in range(2):
                    pe.wait_ge(probs_ready, 3 * gi + b + 1)
                    for kt in range(qt + 1):
                        turn(gi, b, lambda i: zbuf[:, b, i, kt * P:(kt + 1) * P], P)
                pe.wait_ge(probs_ready, 3 * gi + 3)
                turn(gi, 2, lambda i: zbuf_c[:, i, :], N_CMP)
                pe.wait_ge(turned_copied, batches[0])
                if gi > 0:
                    pe.wait_ge(heads_ready, gi)
                else:
                    pe.wait_ge(brow_ready, 1)
                dst = psum[g * HD:(g + 1) * HD, 7, :]
                n = 0
                for b in range(2):
                    for kt in range(qt + 1):
                        pe.matmul(dst, v_tok[:, b, kt, g * HD:(g + 1) * HD], probs_t[:, gi % 2, n, :],
                                  start=(n == 0), stop=False)
                        n += 1
                pe.matmul(dst, v_cmp[0:N_CMP, g * HD:(g + 1) * HD], probs_t[0:N_CMP, gi % 2, n, :],
                          start=False, stop=True).then_inc(heads_sum, 1)

            pe.wait_ge(in1_even, 3 + Z1 // 2)
            pe.wait_ge(in1_odd, 3 + Z1 // 2)
            pe.wait_ge(bias_ready, 6)
            logits(0)
            for gi in range(4):
                if gi < 3:
                    logits(gi + 1)
                attend(gi)

            pe.wait_ge(x_split, X_MIX + 1)
            for m in range(KD):
                slot = tile_split(pe, B_OUT1 + m)
                if m >= 4:
                    pe.wait_ge(out1_ready, m - 3)
                project(slot, psum[:, m % 4, 0:TX], TX).then_inc(tiles_used, 1)
            norm_pe(1, TX, 4)
            norm_pe(2, TX, 5)

            pe.wait_ge(x_split, X_NORM2 + 1)
            pe.wait_ge(zeros_ready, 1)
            zero_y()

            def ffn_up(j, k0, i=None):
                for half in range(2):
                    slot = tile_split(pe, B_FFN + k0 + half, i)
                    bank = 2 * (j % 2) + half
                    if i is not None:
                        pe.wait_ge((ffn_conv_g, ffn_conv_u)[half], i * 2 + (j + 1))
                    else:
                        pe.wait_ge((ffn_conv_g, ffn_conv_u)[half], j + 1)
                    project(slot, psum[:, bank, 0:TX], TX).then_inc(tiles_used, 1)

            def ffn_down(j, k0, i=None):
                slot = tile_split(pe, B_FFN + k0, i)
                pe.wait_ge(hidden_low, j + 1 if i is None else i * 2 + (j + 1))
                return down(slot, j % 2)

            ffn_up(0, 0)
            with pe.Fori(0, (NF - 2) // 2) as i:
                for s in range(2):
                    ffn_up(s + 1, 2 + 3 * s, i)
                    ffn_down(s, 4 + 3 * s, i).then_inc(tiles_used, 1)
            ffn_up(NF - 1, 3 * NF - 4)
            ffn_down(NF - 2, 3 * NF - 2).then_inc(tiles_used, 1)
            ffn_down(NF - 1, 3 * NF - 1).then_inc(tiles_used, 1)
            norm_pe(3, TX, 0)

            norm_pe(4, T2, 7)
            pe.wait_ge(x_split, X_NORM4 + 1)

            def in2(k, i=None):
                slot = tile_split(pe, B_IN2 + k, i)
                pe.wait_ge(in2_copied, trip(k + 1, i))
                project(slot, psum[:, k % BODY, 0:T2], T2).then_inc(tiles_used, 1)

            pieces(B_IN2, 22, pe, in2)

            for r in range(2):
                pe.wait_ge((conv2_ready, cv_squares)[r], 1)
                for k in range(4):
                    mm = pe.matmul(psum[:, 6, 0:T2], const("ones"), (conv_y, sq4)[r][:, k, :], start=(k == 0), stop=(k == 3))
                mm.then_inc(cv_sum, 1)

            pe.wait_ge(second_loaded, 16)
            pe.wait_ge(in2_copied, BODY + 22)
            for n, (lo, hi, w, src) in enumerate(((0, HD, "wa_up", 20), (HD, P, "wa_up", 20), (0, P, "g_up", 21))):
                pe.wait_ge(lowrank_ready, 2)
                for m in range(4):
                    if n == 2:
                        pe.wait_ge(up_ready, m + 1)
                    if n == 1 and m == 2:
                        pe.wait_ge(cv_mean, 2)
                    mm = pe.matmul(psum[:, (4 * n + m) % 8, 0:T2], colv(w, m * P, (m + 1) * P)[lo:hi], z2[lo:hi, src, 1:T2 + 1],
                                   start=True, stop=True)
                    mm.then_inc(up_sum, 1)
            for r, (ready, src) in enumerate(((kk_squares, sq4), (bonus_in, sq4))):
                pe.wait_ge(ready, 1)
                if r == 0:
                    pe.wait_ge(up_ready, 8)
                for m in range(4):
                    mm = pe.matmul(psum[:, 4 + m, 0:T2], const("headones"), src[:, m, :], start=True, stop=True)
                mm.then_inc((kk_sum, bonus_sum)[r], 1)

            pe.wait_ge(up_ready, 12)
            pe.wait_ge(feats_ready, 2)

            def fm(x, h, t0, nt):
                q = slice(h % 2 * HD, (h % 2 + 1) * HD)
                return x[q, h // 2, t0:t0 + nt]

            for tg in range(3):
                t0, nt = tg * P, min(P, T2 - tg * P)
                if tg > 0:
                    pe.wait_ge(o_ready, tg)
                for n, src in enumerate((alpha, z2[:, 16:20, 1:T2 + 1], kappa_end, beta_end)):
                    for m in range(4):
                        mm = pe.transpose(psum[0:nt, n, m * P:(m + 1) * P], src[:, m, t0:t0 + nt], const("ident"))
                    mm.then_inc(tm_sum, 1)
                for hh in range(2):
                    u = 2 * tg + hh
                    pe.wait_ge(tm_ready, 4 * (tg + 1))
                    if u > 0:
                        pe.wait_ge(eo_ready, 2 * u)
                        pe.wait_ge(f_ready, min(2 * u, 8))
                        pe.wait_ge(g_ready, min(2 * u, 8))
                    G = lambda n, h: gram[0:nt, n, h, 0:nt]
                    yh = lambda h, a=0, b=P: ycol[0:nt, h, a:b]
                    tmh = lambda n, h: tm[0:nt, n, (4 * hh + h) * HD:(4 * hh + h + 1) * HD]
                    out = lambda bank, h: psum[0:nt, bank, h * P:h * P + nt]
                    for n, kinds in enumerate((((beta, alpha), (kappa, alpha)), ((alpha, beta),), ((beta, rho), (kappa, rho)))):
                        for odd in range(2):
                            for k, (x, y) in enumerate(kinds):
                                for h in (odd, odd + 2):
                                    mm = pe.matmul(out(2 * n + odd, 2 * k + h // 2), fm(x, 4 * hh + h, t0, nt),
                                                   fm(y, 4 * hh + h, t0, nt), start=True, stop=True)
                            mm.then_inc(gram_sum, 1)

                    def product(bank, a, b, done, rhs=None):
                        for h in range(4):
                            r = G(b, h) if rhs is None else rhs(h)
                            dst = psum[0:nt, bank, h * P:h * P + r.shape[1]]
                            mm = pe.matmul(dst, G(a, h), r, start=True, stop=True)
                        mm.then_inc(done, 1)

                    pe.wait_ge(gram_ready, 6 * u + 4)
                    product(6, G_LT, G_L, pow_sum)
                    product(7, G_L, G_LT, pow_sum)
                    product(1, G_MT, None, mv_sum, lambda h: tmh(1, h))
                    pe.wait_ge(y_ready, 2 * u + 2)
                    product(0, G_LT, None, app_sum, yh)
                    pe.wait_ge(pow_ready, 5 * u + 2)
                    product(2, G_L2T, G_L2, pow_sum)
                    product(3, G_L2, G_L2T, pow_sum)
                    pe.wait_ge(app_ready, 4 * u + 1)
                    product(1, G_L2T, None, app_sum, yh)
                    pe.wait_ge(pow_ready, 5 * u + 4)
                    product(6, G_L4, G_L4T, pow_sum)
                    pe.wait_ge(app_ready, 4 * u + 2)
                    product(0, G_L4T, None, app_sum, yh)
                    pe.wait_ge(pow_ready, 5 * u + 5)
                    pe.wait_ge(app_ready, 4 * u + 3)
                    product(1, G_L8T, None, app_sum, yh)
                    pe.wait_ge(app_ready, 4 * u + 4)
                    pe.wait_ge(gram_ready, 6 * u + 6)
                    for h in range(4):
                        q = slice(h % 2 * HD, (h % 2 + 1) * HD)
                        c = h // 2 * P
                        pe.matmul(psum[q, 4, c:c + nt], yh(h, 0, HD), G(G_QT, h), start=True, stop=True)
                        pe.matmul(psum[q, 5, c:c + nt], tmh(1, h), G(G_RT, h), start=True, stop=False)
                        mm = pe.matmul(psum[q, 5, c:c + nt], yh(h, HD, P), G(G_QT, h), start=False, stop=True)
                    mm.then_inc(eo_sum, 1)
                    if tg < 2:
                        for p in range(2):
                            n = 2 * u + p
                            pe.wait_ge(spread_b, 2 * (n + 1))
                            pe.wait_ge(spread_y, n + 1)
                            if p > 0:
                                pe.wait_ge(f_ready, n)
                                pe.wait_ge(g_ready, n)
                            for x in range(2):
                                h = 2 * p + x
                                q = slice(x * HD, (x + 1) * HD)
                                ex = lambda k: expand[0:nt, k, x].rearrange("p a b -> p (a b)")
                                pe.matmul(psum[q, 6, :], yh(h, 0, HD), ex(0), start=True, stop=True)
                                pe.matmul(psum[q, 7, :], tmh(2, h), ex(1), start=True, stop=False)
                                mm = pe.matmul(psum[q, 7, :], tmh(3, h), ex(2), start=False, stop=True)
                            mm.then_inc(fg_sum, 1)
                if tg < 2:
                    pe.wait_ge(f_ready, 4 * (tg + 1))
                    pe.wait_ge(g_ready, 4 * (tg + 1))
                pe.wait_ge(eo_ready, 4 * (tg + 1))
                for c in range(nt // CH):
                    slot = 8 if tg and c == 0 else c
                    pe.wait_ge(state_ready, 8 * tg + c + 1)
                    for h in range(8):
                        q = slice(h % 2 * HD, (h % 2 + 1) * HD)
                        s = state[q, h // 2, slot, :]
                        mm = pe.matmul(psum[q, 2, h // 2 * P + c * CH:h // 2 * P + (c + 1) * CH], s,
                                       e_t[q, h // 2, c * CH:(c + 1) * CH], start=True, stop=True)
                    if tg < 2:
                        for h in range(8):
                            q = slice(h % 2 * HD, (h % 2 + 1) * HD)
                            mm = pe.matmul(psum[q, c % 2, h // 2 * HD:(h // 2 + 1) * HD], f_t[q, h // 2, c, :],
                                           state[q, h // 2, slot, :], start=True, stop=True)
                    mm.then_inc(rec_sum, 1)

            for r in range(2):
                if r == 0:
                    pe.wait_ge(o_ready, 3)
                else:
                    pe.wait_ge(gn_sq, 1)
                for m in range(4):
                    mm = pe.matmul(psum[:, 4 * r + m, 0:T2], const("headones"), (o_all, gn_s)[r][:, m, :], start=True, stop=True)
                mm.then_inc(gn_sum, 1)

            for g in range(16):
                slot = tile_split(pe, B_MID + g)
                if g >= 4:
                    pe.wait_ge(gate_sig, g - 3)
                project(slot, psum[:, g % 4, 0:TX], TX, t0=N_META).then_inc(tiles_used, 1)
            pe.wait_ge(x_split, X_BRANCH + 1)
            pe.wait_ge(gate_sig, 16)
            for m in range(KD):
                if m >= 4:
                    pe.wait_ge(merged_ready, m - 3)
                slot = tile_split(pe, B_MID + 16 + m)
                b0 = 2 * (m % 4)
                project(slot, psum[:, b0, 0:TX], TX, range(4))
                project(slot, psum[:, b0 + 1, 0:TX], TX, range(4, 8)).then_inc(tiles_used, 1)
            pe.wait_ge(x_split, X_MERGED + 1)
            for m in range(KD):
                slot = tile_split(pe, B_OUT2 + m)
                project(slot, psum[:, m, 0:TX], TX).then_inc(tiles_used, 1)
            pe.wait_ge(out2_added, KD)
            norm_pe(5, TX, 6)
            pe.wait_ge(x_split, X_NORM5 + 1)

            for m in range(16):
                slot = tile_split(pe, B_Q + m)
                if m >= 4:
                    pe.wait_ge(q_copied, m - 3)
                project(slot, psum[:, m % 4, 0:TX], TX).then_inc(tiles_used, 1)
            for n in range(2):
                slot = tile_split(pe, B_SUB + n)
                if n == 0:
                    pe.wait_ge(q_copied, 16)
                for qt in range(2):
                    if n == 1:
                        pe.wait_ge(score_copied, 2 * qt + 2)
                    for k in range(8):
                        for p, w in enumerate((w_hi, w_lo)):
                            mm = pe.matmul(psum[:, 4 * qt + k // 4 + 0, (k % 4) * P:(k % 4 + 1) * P],
                                           query[:, 8 * n + k, qt * P:(qt + 1) * P], w[:, slot, k * P:(k + 1) * P].bitcast(F32),
                                           start=(p == 0), stop=(p == 1))
                        if k % 4 == 3 and not (qt == 1 and k == 7):
                            mm.then_inc(score_sum, 1)
                mm.then_inc(tiles_used, 1)
            pe.wait_ge(score_copied, 8)

            def expert_up(e, i=None):
                slot = tile_split(pe, B_EXP + e, i)
                pe.wait_ge(expert_act, trip(e + 1, i))
                project(slot, psum[:, e % BODY, 0:TX], TX).then_inc(tiles_used, 1)

            pieces(B_EXP, NE, pe, expert_up)

            pe.wait_ge(chosen_ready, 2)
            for n in range(3):
                for qt in range(2):
                    mm = pe.transpose(psum[:, 6 + n // 2, (n % 2) * TX + qt * P:(n % 2) * TX + (qt + 1) * P],
                                      chosen[:, n, qt].rearrange("p a b -> p (a b)"), const("ident"))
            mm.then_inc(chosen_sum, 1)

            pe.wait_ge(expert_act, BODY + NE)
            with pe.Fori(0, TX // 8) as i:
                for s in range(2):
                    pe.wait_ge(hot_a, i * 2 + (s + 1))
                    pe.wait_ge(hot_b, i * 2 + (s + 1))
                    pe.wait_ge(gates_used, i * 2 + (s + 1))
                    for t in range(4):
                        mm = pe.matmul(psum[:, s, t * P:(t + 1) * P], hot_1[:, s, t, :], hot_2[:, s, t, :].bitcast(F32), start=True, stop=True)
                    mm.then_inc(gates_done, 1)

            zero_y()

            def expert_down(e, i=None):
                slot = tile_split(pe, B_V + e, i)
                pe.wait_ge(coef_low, trip(e + 1, i))
                down(slot, e % 2).then_inc(tiles_used, 1)

            pieces(B_V, NE, pe, expert_down)
            norm_pe(6, TX, 0)

        exp_turn = []

        @block.vector
        def _(dve):
            steps = [0]

            def step(ins):
                steps[0] += 1
                ins.then_inc(dve_step, 1)
                dve.wait_ge(dve_step, steps[0])

            def norm_scale(n, width, bank, total=D, eps=EPS):
                dve.wait_ge(norm_sums, n + 1)
                dve.tensor_scalar(rms[:, 0:width], psum[:, bank, 0:width], 1.0 / total, eps,
                                  ALU.mult, ALU.add).then_inc(norm_mean, 1)
                dve.wait_ge(norm_root, n + 1)
                step(dve.reciprocal(rms[:, 0:width], rms[:, 0:width]))

            def norm_pre(n, src, width, bank, gain, done=norm_part):
                norm_scale(n, width, bank)
                for k in range(KD):
                    ins = dve.scalar_tensor_tensor(out=sq[:, k, 0:width], in0=src[:, k, :], scalar=colv(gain, k, k + 1),
                                                   in1=rms[:, 0:width], op0=ALU.mult, op1=ALU.mult)
                    if done is norm_part and k % 2:
                        ins.then_inc(norm_part, 1)
                if done is not norm_part:
                    ins.then_inc(done, 1)

            def low_x(s, src):
                for q in range(4):
                    dve.wait_ge(high_part, 4 * s + q + 1)
                    x = src(q)
                    w = x.shape[2]
                    ins = dve.tensor_tensor(x_lo[:, 2 * q:2 * q + 2, 0:w], x, x_hi[:, 2 * q:2 * q + 2, 0:w].bitcast(F32), ALU.subtract)
                ins.then_inc(x_split, 1)

            def low_norm(s, width):
                low_x(s, lambda q: sq[:, 2 * q:2 * q + 2, 0:width])

            def norm_post(n, y, width, bank, gain):
                norm_scale(n, width, bank)
                step(dve.tensor_tensor(y, y, rms[:, 0:width].unsqueeze(1).to_broadcast([P, KD, width]), ALU.mult))
                for k in range(KD):
                    ins = dve.scalar_tensor_tensor(out=hx1[:, k, :], in0=y[:, k, :], scalar=colv(gain, k, k + 1),
                                                   in1=hx1[:, k, :], op0=ALU.mult, op1=ALU.add)
                ins.then_inc(norm_out, 1)

            dve.wait_ge(brow_sum, 1)
            dve.tensor_copy(brow[0:N_HEADS, :], psum[0:N_HEADS, 7, :]).then_inc(brow_ready, 1)
            dve.wait_ge(param_loaded, 16)
            dve.wait_ge(x_loaded, 16)
            norm_pre(0, hx1, TX, 6, "mix_pre")
            split_low(dve, 0)
            low_norm(X_NORM0, TX)
            split_low(dve, 1)
            dve.sem_inc(in1_even, 3)
            with dve.Fori(0, Z1 // BODY) as i:
                for k in range(BODY):
                    split_low(dve, B_IN1 + k + 2, i)
                    if k % 2 == 0:
                        dve.wait_ge(tiles_used, i * BODY + (B_IN1 + k + 1))
                        dve.tensor_copy(z1[:, i * BODY + k, :], psum[:, k, 0:TX]).then_inc(in1_even, 1)
            dve.wait_ge(first_loaded, 16)
            dve.wait_ge(in1_odd, 3 + Z1 // 2)
            dve.wait_ge(in1_even, 3 + Z1 // 2)

            for kv in range(2):
                for g in range(N_KV):
                    for half in range(2):
                        q = slice(half * HD, (half + 1) * HD)
                        src = z1[q, ZKC + 2 * kv + g, half * 16:half * 16 + 16 * N_CMP].rearrange("p (n r) -> p r n", r=16)
                        ins = dve.tensor_tensor(cmp_in[q, kv, :, g * N_CMP:(g + 1) * N_CMP], src,
                                                colv("pe", kv * 16, kv * 16 + 16)[q].unsqueeze(2).to_broadcast([HD, 16, N_CMP]),
                                                ALU.add)
            ins.then_inc(cmp_blocks, 1)
            for j in range(8):
                split_low(dve, B_CMP + j + 2)
            dve.wait_ge(vtok_sum, 1)
            dve.tensor_copy(v_tok.rearrange("p a b c -> p (a b c)"), psum[:, 4, :]).then_inc(vtok_ready, 1)
            dve.wait_ge(cmp_sum, 1)
            dve.tensor_copy(k_cmp[0:HD, :], psum[0:HD, 5, 0:N_CMP]).then_inc(cmp_ready, 1)
            dve.tensor_copy(k_cmp[HD:P, :], psum[HD:P, 5, N_CMP:2 * N_CMP]).then_inc(cmp_ready, 1)
            dve.tensor_copy(v_cmp[0:N_CMP, :], psum[0:N_CMP, 5, 64:64 + P]).then_inc(cmp_ready, 1)

            def short_conv():
                step(dve.tensor_tensor(conv_m, z1[:, ZC:ZC + 4, :], z1[:, ZX:ZX + 4, :], ALU.mult))
                for t in range(4):
                    ins = dve.tensor_scalar(mix[:, 4 + t, :], conv_m[:, t, :], colv("conv_mix", 3 * t + 2, 3 * t + 3),
                                            None, ALU.mult)
                step(ins)
                for back in (1, 2):
                    for t in range(4):
                        ins = dve.scalar_tensor_tensor(out=mix[:, 4 + t, back:TX], in0=conv_m[:, t, 0:TX - back],
                                                       scalar=colv("conv_mix", 3 * t + 2 - back, 3 * t + 3 - back),
                                                       in1=mix[:, 4 + t, back:TX], op0=ALU.mult, op1=ALU.add)
                    step(ins)
                dve.tensor_tensor(mix[:, 4:8, :], mix[:, 4:8, :], z1[:, ZB:ZB + 4, :], ALU.mult).then_inc(conv_ready, 1)

            def shift_max(z, bias, bank_ap, n):
                step(dve.scalar_tensor_tensor(out=z, in0=bank_ap, scalar=SCALE, in1=bias, op0=ALU.mult, op1=ALU.add))
                step(dve.tensor_reduce(red[:, 0, 0:REP], z, AX, ALU.max))
                dve.tensor_tensor(z, z, red[:, 0, 0:REP].unsqueeze(2).to_broadcast([P, REP, n]),
                                  ALU.subtract).then_inc(logits_ready, 1)

            def gated(z, branch, qt, g, n, mask=None):
                step(dve.tensor_reduce(red[:, 1, 0:REP], z, AX, ALU.add))
                step(dve.reciprocal(red[:, 1, 4:8], red[:, 1, 0:REP]))
                f = red[:, 1, 8:12]
                step(dve.tensor_tensor(f, red[:, 1, 4:8], gates[:, qt, branch * 8 + 4 * g:branch * 8 + 4 * g + 4], ALU.mult))
                if mask is not None:
                    step(dve.tensor_scalar(red[:, 1, 12:16], f, mask, None, ALU.mult))
                    f = red[:, 1, 12:16]
                dve.tensor_tensor(z, z, f.unsqueeze(2).to_broadcast([P, REP, n]), ALU.mult).then_inc(probs_ready, 1)

            dve.wait_ge(bias_ready, 6)
            dve.wait_ge(gates_ready, 1)
            turns = 0
            for gi in range(4):
                qt, g = gi // 2, gi % 2
                nk = P * (qt + 1)
                heads = slice(4 * g, 4 * g + 4)
                for b in range(2):
                    dve.wait_ge(logits_sum, 3 * gi + b + 1)
                    if gi > 0 and b == 0:
                        dve.wait_ge(turned, turns)
                    bank = psum[:, 2 * b:2 * b + 2, :].rearrange("p a (c k) -> p (a c) k", c=2)
                    shift_max(zbuf[:, b, :, 0:nk], bias_t[:, heads, TX - nk:TX], bank[:, :, 0:nk], nk)
                dve.wait_ge(logits_sum, 3 * gi + 3)
                shift_max(zbuf_c, bias_t[:, heads, 159 - qt * P:159 - qt * P + 16 * N_CMP - 15:16],
                          psum[:, 4, 0:64].rearrange("p (a b) -> p a b", a=REP)[:, :, 0:N_CMP], N_CMP)
                if gi == 0:
                    short_conv()
                for b in range(2):
                    dve.wait_ge(exps_ready, 3 * gi + b + 1)
                    gated(zbuf[:, b, :, 0:nk], 1 + b, qt, g, nk)
                dve.wait_ge(exps_ready, 3 * gi + 3)
                gated(zbuf_c, 0, qt, g, N_CMP, const("rowmask")[:, qt:qt + 1])
                turns += 2 * (qt + 1) + 1

            low_x(X_MIX, lambda q: mix[:, 2 * q:2 * q + 2, :])
            for m in range(KD):
                split_low(dve, B_OUT1 + m + 2)
            norm_post(1, y1, TX, 4, "mix_post")
            norm_pre(2, hx1, TX, 5, "ffn_pre")
            low_norm(X_NORM2, TX)

            dve.sem_inc(ffn_conv_g, 2)
            dve.sem_inc(ffn_conv_u, 2)

            def ffn_dve(j, i=None):
                def trips(per, v):
                    return v if i is None else i * per + v

                par = j % 2
                at = FIRST["ffn_conv"][0] + 6 * j
                src = first_sb[:, at:at + 6] if i is None else first_sb[:, bass.ds(i * 12 + at, 6)]
                dve.tensor_copy(taps[:, par, :], src).then_inc(ffn_taps, 1)
                dve.wait_ge(ffn_taps, trips(2, j + 1))
                for half, done in ((0, ffn_conv_g), (1, ffn_conv_u)):
                    split_low(dve, B_FFN + (3 * j + 1 if j else 2) + half, i)
                    dve.wait_ge(ffn_scaled, trips(4, 2 * j + half + 1))
                    c = ffn_c[:, par, half, :]
                    for back in (1, 2):
                        ins = dve.scalar_tensor_tensor(out=c[:, back:TX], in0=psum[:, 2 * par + half, 0:TX - back],
                                                       scalar=taps[:, par, 3 * half + 2 - back:3 * half + 3 - back],
                                                       in1=c[:, back:TX], op0=ALU.mult, op1=ALU.add)
                        if back == 1:
                            ins.then_inc(ffn_mid, 1)
                            dve.wait_ge(ffn_mid, trips(4, 2 * j + half + 1))
                        else:
                            ins.then_inc(done, 1)
                dve.wait_ge(ffn_gelu, trips(2, j + 1))
                dve.wait_ge(ffn_conv_u, trips(2, j + 3))
                dve.tensor_tensor(ffn_h[:, par, :], ffn_g[:, par, :], ffn_c[:, par, 1, :], ALU.mult).then_inc(ffn_whole, 1)
                if j > 0:
                    split_low(dve, B_FFN + 3 * j + 3, i)
                dve.wait_ge(hidden_high, trips(2, j + 1))
                dve.tensor_tensor(h_lo[:, par, :], ffn_h[:, par, :], h_hi[:, par, :].bitcast(F32), ALU.subtract).then_inc(hidden_low, 1)

            ffn_dve(0)
            with dve.Fori(0, (NF - 2) // 2) as i:
                ffn_dve(1, i)
                ffn_dve(2, i)
            ffn_dve(NF - 1)
            split_low(dve, B_FFN + 3 * NF + 1)
            norm_post(3, y1, TX, 0, "ffn_post")

            norm_pre(4, hx, T2, 7, "mix2")
            low_norm(X_NORM4, T2)
            with dve.Fori(0, 2) as i:
                for k in range(BODY):
                    split_low(dve, B_IN2 + k + 2, i)
            zs = z2[:, :, 1:T2 + 1]

            dve.wait_ge(pads_zeroed, 2)
            dve.wait_ge(glu_sig, 1)
            step(dve.tensor_tensor(glu[:, :, TAPS - 1:], zs[:, 0:4], zs[:, 4:8], ALU.mult))
            dve.wait_ge(second_loaded, 16)
            for m in range(4):
                ins = dve.tensor_scalar(conv_y[:, m, :], glu[:, m, 0:T2], colv("conv_w", m * TAPS, m * TAPS + 1),
                                        colv("conv_b", m, m + 1), ALU.mult, ALU.add)
            for t in range(1, TAPS):
                if 12 + t - 1 < 22:
                    split_low(dve, B_IN2 + 12 + t - 1 + 2)
                for m in range(4):
                    if m % 2 == 0:
                        step(ins)
                    ins = dve.scalar_tensor_tensor(out=conv_y[:, m, :], in0=glu[:, m, t:t + T2],
                                                   scalar=colv("conv_w", m * TAPS + t, m * TAPS + t + 1),
                                                   in1=conv_y[:, m, :], op0=ALU.mult, op1=ALU.add)
            ins.then_inc(conv2_ready, 1)
            dve.wait_ge(cv_sum, 1)
            dve.tensor_scalar(rms[:], psum[:, 6, 0:T2], 1.0 / 512, None, ALU.mult).then_inc(cv_mean, 1)
            dve.wait_ge(cv_mean, 1)
            dve.tensor_tensor(conv_y, conv_y, rms[:].unsqueeze(1).to_broadcast([P, 4, T2]),
                              ALU.subtract).then_inc(cv_diff, 1)

            dve.wait_ge(in2_copied, BODY + 22)
            step(dve.tensor_tensor(delta, z2[:, 8:22, 0:T2], zs[:, 8:22], ALU.subtract))
            for n in range(14):
                ins = dve.scalar_tensor_tensor(out=zs[:, 8 + n, :], in0=delta[:, n, :], scalar=colv("mu", n, n + 1),
                                               in1=zs[:, 8 + n, :], op0=ALU.mult, op1=ALU.add)
            ins.then_inc(shifted, 1)
            dve.wait_ge(cv_sum, 2)
            dve.tensor_scalar(rms[:], psum[:, 6, 0:T2], 1.0 / 512, LN_EPS, ALU.mult, ALU.add).then_inc(cv_mean, 1)
            dve.wait_ge(cv_root, 1)
            step(dve.reciprocal(rms[:], rms[:]))
            dve.tensor_tensor(conv_y, conv_y, rms[:].unsqueeze(1).to_broadcast([P, 4, T2]),
                              ALU.mult).then_inc(cv_scaled, 1)

            r_z, k_z, v_z = zs[:, 8:12], zs[:, 12:16], zs[:, 16:20]
            dve.wait_ge(shifted, 1)
            for m in range(4):
                ins = dve.tensor_scalar(kk[:, m, :], k_z[:, m, :], colv("k_k", m, m + 1), None, ALU.mult)
            ins.then_inc(kk_raw, 1)
            flat = lambda v: v.rearrange("p a b -> p (a b)")
            chunks = lambda v: v.rearrange("p a (c s) -> p (a c) s", s=CH)
            dve.wait_ge(up_ready, 4)
            step(dve.tensor_scalar(logdec, logdec, -float(np.exp(-0.5)), None, ALU.mult))
            for m in range(4):
                ins = dve.tensor_tensor_scan(cum[:, m, :], const("scanmask"), logdec[:, m, :], 0.0, ALU.mult, ALU.add)
            step(ins)
            dve.tensor_tensor(e_prev, cum, logdec, ALU.subtract)
            dve.tensor_tensor(chunks(e_end), chunks(cum)[:, :, CH - 1:CH].to_broadcast([P, 4 * NCH, CH]), chunks(cum),
                              ALU.subtract).then_inc(cums_ready, 1)
            dve.wait_ge(kk_sum, 1)
            dve.tensor_scalar(k_new, psum[:, 4:8, 0:T2], 1e-24, None, ALU.max).then_inc(kk_mean, 1)
            dve.wait_ge(kk_root, 1)
            step(dve.reciprocal(b_vec, k_new))
            step(dve.tensor_tensor(kk, kk, b_vec, ALU.mult))
            dve.wait_ge(up_ready, 8)
            for m in range(4):
                ins = dve.tensor_scalar(k_new[:, m, :], a_gate[:, m, :], -1.0, colv("k_a", m, m + 1), ALU.add, ALU.mult)
            step(ins)
            dve.tensor_tensor(b_vec, kk, a_gate, ALU.mult)
            step(dve.scalar_tensor_tensor(out=k_new, in0=k_new, scalar=1.0, in1=k_z, op0=ALU.add, op1=ALU.mult))
            step(dve.tensor_tensor(sq4, r_z, k_new, ALU.mult))
            for m in range(4):
                ins = dve.tensor_scalar(sq4[:, m, :], sq4[:, m, :], colv("r_k", m, m + 1), None, ALU.mult)
            ins.then_inc(bonus_in, 1)
            dve.wait_ge(cexp_ready, 5)
            dve.tensor_tensor(alpha, kk, e_prev, ALU.mult)
            dve.scalar_tensor_tensor(out=beta, in0=b_vec, scalar=-1.0, in1=e_neg, op0=ALU.mult, op1=ALU.mult)
            dve.scalar_tensor_tensor(out=beta_end, in0=b_vec, scalar=-1.0, in1=e_end, op0=ALU.mult, op1=ALU.mult)
            dve.tensor_tensor(kappa, k_new, e_neg, ALU.mult)
            dve.tensor_tensor(kappa_end, k_new, e_end, ALU.mult)
            dve.tensor_tensor(rho, r_z, e_cum, ALU.mult).then_inc(feats_ready, 1)
            dve.wait_ge(bonus_sum, 1)
            dve.tensor_tensor(bonus, psum[:, 4:8, 0:T2], v_z, ALU.mult).then_inc(feats_ready, 1)

            for tg in range(3):
                t0, nt = tg * P, min(P, T2 - tg * P)
                for hh in range(2):
                    u = 2 * tg + hh
                    for n, (dst, kinds, mask) in enumerate(((G_LT, 2, "upper"), (G_L, 1, "lower"), (G_QT, 2, "upper_in"))):
                        for odd in range(2):
                            dve.wait_ge(gram_sum, 6 * u + 2 * n + odd + 1)
                            dve.tensor_tensor(gram[0:nt, dst:dst + kinds, odd::2, 0:nt],
                                              psum[0:nt, 2 * n + odd, 0:kinds * 2 * P].rearrange("p (k h t) -> p k h t", k=kinds, h=2)[:, :, :, 0:nt],
                                              const(mask)[0:nt, 0:nt].unsqueeze(1).unsqueeze(1).to_broadcast([nt, kinds, 2, nt]),
                                              ALU.mult).then_inc(gram_ready, 1)
                    for j in range(4):
                        dve.wait_ge(app_sum, 4 * u + j + 1)
                        if j > 0:
                            dve.wait_ge(app_ready, 4 * u + j)
                        dve.tensor_tensor(ycol[0:nt], by_head(psum[0:nt, j % 2, :]), ycol[0:nt],
                                          ALU.add).then_inc(app_ready, 1)
                    two = lambda v: v.rearrange("p (a b) -> p a b", a=4)[:, 0:2, 0:nt]
                    dve.wait_ge(eo_sum, u + 1)
                    dve.tensor_tensor(e_t[:, 2 * hh:2 * hh + 2, 0:nt], two(psum[:, 4, :]), rho[:, 2 * hh:2 * hh + 2, t0:t0 + nt],
                                      ALU.add).then_inc(eo_ready, 1)
                    dve.tensor_copy(o_in[:, 2 * hh:2 * hh + 2, 0:nt], two(psum[:, 5, :])).then_inc(eo_ready, 1)
                    if tg < 2:
                        for p in range(2):
                            n = 2 * u + p
                            if n > 0:
                                dve.wait_ge(fg_sum, n)
                            dve.wait_ge(app_ready, 4 * u + 4)
                            dve.tensor_tensor(expand[:, 2], ycol[:, 2 * p:2 * p + 2, HD:P].unsqueeze(2).to_broadcast([P, 2, 8, HD]),
                                              const("chunk").unsqueeze(1).unsqueeze(3).to_broadcast([P, 2, 8, HD]),
                                              ALU.mult).then_inc(spread_y, 1)
                            dve.wait_ge(fg_sum, n + 1)
                            dve.wait_ge(decay_diag, tg + 1)
                            ft = f_t[:, 2 * hh + p].rearrange("p a b -> p (a b)")
                            dve.tensor_tensor(ft, psum[:, 6, :], ft, ALU.add).then_inc(f_ready, 1)
                if tg < 2:
                    dve.wait_ge(g_ready, 4 * (tg + 1))
                    for c in range(8):
                        dve.wait_ge(rec_sum, 8 * tg + c + 1)
                        dve.tensor_tensor(state[:, :, c + 1, :], psum[:, c % 2, 0:4 * HD].rearrange("p (a b) -> p a b", a=4),
                                          g_c[:, :, c, :], ALU.add).then_inc(state_ready, 1)
                else:
                    dve.wait_ge(rec_sum, NCH)
                dve.wait_ge(eo_ready, 4 * (tg + 1))
                dve.tensor_tensor(o_all[:, :, t0:t0 + nt], by_head(psum[:, 2, :])[:, :, 0:nt], o_in[:, :, 0:nt],
                                  ALU.add).then_inc(o_ready, 1)

            dve.wait_ge(gn_sum, 1)
            dve.wait_ge(o_ready, 3)
            step(dve.scalar_tensor_tensor(out=gn_d, in0=psum[:, 0:4, 0:T2], scalar=-1.0 / HD, in1=o_all,
                                          op0=ALU.mult, op1=ALU.add))
            dve.tensor_tensor(gn_s, gn_d, gn_d, ALU.mult).then_inc(gn_sq, 1)
            split_low(dve, B_MID + 2)
            dve.wait_ge(gn_sum, 2)
            dve.tensor_scalar(gn_s, psum[:, 4:8, 0:T2], 1.0 / HD, GN_EPS, ALU.mult, ALU.add).then_inc(gn_mean, 1)
            dve.wait_ge(gn_root, 1)
            step(dve.reciprocal(gn_s, gn_s))
            split_low(dve, B_MID + 3)
            step(dve.tensor_tensor(gn_d, gn_d, gn_s, ALU.mult))
            split_low(dve, B_MID + 4)
            for m in range(4):
                ins = dve.tensor_scalar(gn_d[:, m, :], gn_d[:, m, :], colv("gn_g", m, m + 1), colv("gn_b", m, m + 1),
                                        ALU.mult, ALU.add)
            step(ins)
            split_low(dve, B_MID + 5)
            step(dve.tensor_tensor(gn_d, gn_d, bonus, ALU.add))
            split_low(dve, B_MID + 6)
            dve.tensor_tensor(mid, gn_d[:, :, N_META:T2], gmul[:, :, N_META:T2], ALU.mult).then_inc(mid_ready, 1)
            for g in range(5, 16):
                split_low(dve, B_MID + g + 2)
            low_x(X_BRANCH, branch_in)

            for m in range(KD):
                split_low(dve, B_MID + 16 + m + 2)
                b0 = 2 * (m % 4)
                dve.wait_ge(tiles_used, B_MID + 16 + m + 1)
                dve.wait_ge(gate_sig, 16)
                gates2 = z2[:, m:m + 9:8, 1:TX + 1]
                step(dve.tensor_tensor(part[:, m % 2], gates2, psum[:, b0:b0 + 2, 0:TX], ALU.mult))
                dve.tensor_tensor(merged[:, m, :], part[:, m % 2, 0, :], part[:, m % 2, 1, :], ALU.add).then_inc(merged_ready, 1)
            low_x(X_MERGED, lambda q: merged[:, 2 * q:2 * q + 2, :])
            for m in range(KD):
                split_low(dve, B_OUT2 + m + 2)
                dve.wait_ge(tiles_used, B_OUT2 + m + 1)
                dve.tensor_tensor(hx1[:, m, :], psum[:, m, 0:TX], hx1[:, m, :], ALU.add).then_inc(out2_added, 1)
            dve.wait_ge(out2_added, KD)
            norm_pre(5, hx1, TX, 6, "ffn2")

            low_norm(X_NORM5, TX)
            for m in range(18):
                split_low(dve, B_Q + m + 2)

            turn = [2]

            def tile_between():
                split_low(dve, B_EXP + turn[0])
                turn[0] += 1

            def sixteen(n, values, src, index):
                every = 6 if n == 16 else 4

                def over(j):
                    if j % every == every - 1:
                        tile_between()

                for j in range(n):
                    ins = dve.max(values[:, j, 0:8], src[:, j, :])
                    over(j)
                step(ins)
                for j in range(n):
                    dve.max_index(index[:, j, 0:8], values[:, j, 0:8], src[:, j, :])
                    ins = dve.match_replace(src[:, j, :], values[:, j, 0:8], src[:, j, :], -3e38)
                    over(2 * j + 1)
                step(ins)
                for j in range(n):
                    ins = dve.max(values[:, j, 8:16], src[:, j, :])
                    over(j)
                step(ins)
                for j in range(n):
                    ins = dve.max_index(index[:, j, 8:16], values[:, j, 8:16], src[:, j, :])
                    over(j)
                step(ins)

            dve.wait_ge(score_copied, 8)
            full = [P, 8, TOPK, TOPK]
            for qt in range(2):
                sixteen(16, best, score[:, qt], best_u)
                dve.tensor_copy(best_i, best_u)
                bh = best.rearrange("p (h c) k -> p h c k", c=2)
                step(dve.tensor_tensor(cand, bh[:, :, 0, :].unsqueeze(3).to_broadcast(full),
                                       bh[:, :, 1, :].unsqueeze(2).to_broadcast(full), ALU.add))
                tile_between()
                sixteen(8, pick_s, cand.rearrange("p h a b -> p h (a b)"), pick_u)
                dve.tensor_single_scalar(pick_hi_u, pick_u, 4, ALU.logical_shift_right)
                step(dve.tensor_single_scalar(pick_lo_u, pick_u, 15, ALU.bitwise_and))
                dve.tensor_copy(pick_k[:, 0], pick_hi_u)
                dve.tensor_copy(pick_k[:, 1], pick_lo_u)
                step(dve.tensor_copy(soft[:, 0], pick_s[:, :, 0]))
                dve.tensor_tensor(pick_s, pick_s, soft[:, 0].unsqueeze(2).to_broadcast([P, 8, TOPK]),
                                  ALU.subtract).then_inc(pick_shift, 1)
                exp_turn.append(turn[0])
                ih = best_i.rearrange("p (h c) k -> p h c k", c=2)
                for c in range(2):
                    tile_between()
                    step(dve.tensor_tensor(sel_eq, pick_k[:, c].unsqueeze(3).to_broadcast(full),
                                           const("iota")[:, 0:TOPK].unsqueeze(1).unsqueeze(1).to_broadcast(full), ALU.is_equal))
                    tile_between()
                    step(dve.tensor_tensor(sel_eq, sel_eq, ih[:, :, c, :].unsqueeze(2).to_broadcast(full), ALU.mult))
                    tile_between()
                    step(dve.tensor_reduce(chosen[:, 1 + c, qt], sel_eq, AX, ALU.add))
                tile_between()
                dve.wait_ge(pick_exp, qt + 1)
                step(dve.tensor_reduce(soft[:, 0], pick_s, AX, ALU.add))
                step(dve.reciprocal(soft[:, 1], soft[:, 0]))
                dve.tensor_tensor(chosen[:, 0, qt], pick_s, soft[:, 1].unsqueeze(2).to_broadcast([P, 8, TOPK]),
                                  ALU.mult).then_inc(chosen_ready, 1)
                dve.wait_ge(chosen_ready, qt + 1)
            assert turn[0] < FREE_EXPERTS + 2
            rest = NE + 2 - turn[0]
            at0 = turn[0]
            pieces(B_EXP, rest, dve, lambda k, i: split_low(dve, B_EXP + at0 + k, i))

            dve.wait_ge(chosen_sum, 1)
            dve.tensor_copy(chosen_t[:, 0, :], psum[:, 6, 0:TX]).then_inc(chosen_turned, 1)
            dve.tensor_scalar(chosen_t[:, 1, :], psum[:, 6, 0:TX], -1.0, None, ALU.mult).then_inc(chosen_turned, 1)
            dve.tensor_copy(chosen_t[:, 2, :], psum[:, 6, TX:2 * TX]).then_inc(chosen_turned, 1)
            dve.tensor_copy(chosen_t[:, 3, :], psum[:, 7, 0:TX]).then_inc(chosen_turned, 1)
            dve.wait_ge(chosen_turned, 4)

            def hots(n, i=None):
                t0 = 4 * n if i is None else i * 8 + 4 * n
                s = n % 2
                dve.tensor_tensor(hot_2[:, s], const("iota").unsqueeze(1).to_broadcast([P, 4, NE]),
                                  chosen_t[:, 3, bass.ds(t0, 4)].unsqueeze(2).to_broadcast([P, 4, NE]), ALU.is_equal)
                dve.tensor_scalar(hot_1[:, s, 3, :], const("iota"), chosen_t[:, 2, bass.ds(t0 + 3, 1)],
                                  chosen_t[:, 0, bass.ds(t0 + 3, 1)], ALU.is_equal, ALU.mult).then_inc(hot_b, 1)

            def gated_acts(n, i=None):
                t0 = 4 * n if i is None else i * 8 + 4 * n
                dve.wait_ge(gates_done, n + 1 if i is None else i * 2 + (n + 1))
                a = act_all[:, :, bass.ds(t0, 4)].rearrange("p e t -> p t e")
                dve.tensor_tensor(a, psum[:, n % 2, :].rearrange("p (t e) -> p t e", t=4), a, ALU.mult).then_inc(gates_used, 1)

            dve.sem_inc(gates_used, 2)
            hots(0)
            with dve.Fori(0, TX // 8 - 1) as i:
                for s in range(2):
                    hots(s + 1, i)
                    gated_acts(s, i)
            hots(TX // 4 - 1)
            gated_acts(TX // 4 - 2)
            gated_acts(TX // 4 - 1)

            def low_coef(e, i=None):
                dve.wait_ge(coef_high, trip(e + 1, i))
                dve.tensor_tensor(h_lo[:, e % 2, :], act_all[:, trip(e, i), :], h_hi[:, e % 2, :].bitcast(F32),
                                  ALU.subtract).then_inc(coef_low, 1)

            low_coef(0)
            low_coef(1)
            split_low(dve, B_V + 2)

            def second(k, i=None):
                low_coef(k + 2, i)
                split_low(dve, B_V + k + 3, i)

            pieces(B_V, NE - 3, dve, second)
            low_coef(NE - 1)
            dve.wait_ge(tiles_used, B_V + NE)
            for m in range(4):
                dve.tensor_tensor(hx1[:, 2 * m:2 * m + 2, :], psum[:, 4 + m, :].rearrange("p (a b) -> p a b", a=2),
                                  hx1[:, 2 * m:2 * m + 2, :], ALU.add).then_inc(out3_added, 1)
            dve.wait_ge(out3_added, 4)
            norm_pre(6, hx1, TX, 0, "final", norm_out)

        @block.scalar
        def _(act):
            def norm_act(n, src, width, ready):
                ready()
                act.activation(sq[:, :, 0:width], src, ACT.Square).then_inc(norm_squares, 1)

            def norm_root_act(n, width):
                act.wait_ge(norm_mean, n + 1)
                act.activation(rms[:, 0:width], rms[:, 0:width], ACT.Sqrt).then_inc(norm_root, 1)

            def high_x(s, src, ready=None):
                for q in range(4):
                    if ready is not None:
                        ready(q)
                    x = src(q)
                    act.activation(x_hi[:, 2 * q:2 * q + 2, 0:x.shape[2]], x, ACT.Copy).then_inc(high_part, 1)

            def high_norm(s, n, width):
                high_x(s, lambda q: sq[:, 2 * q:2 * q + 2, 0:width], lambda q: act.wait_ge(norm_part, 4 * n + q + 1))

            norm_act(0, hx1, TX, lambda: act.wait_ge(x_loaded, 16))
            norm_root_act(0, TX)
            split_high(act, 0)
            high_norm(X_NORM0, 0, TX)
            split_high(act, 1)
            act.sem_inc(in1_odd, 3)
            with act.Fori(0, Z1 // BODY) as i:
                for k in range(BODY):
                    split_high(act, B_IN1 + k + 2, i)
                    if k % 2:
                        act.wait_ge(tiles_used, i * BODY + (B_IN1 + k + 1))
                        act.activation(z1[:, i * BODY + k, :], psum[:, k, 0:TX], ACT.Copy).then_inc(in1_odd, 1)
            act.wait_ge(gates_sum, 1)
            act.activation(gates, psum[:, 6, 0:48].rearrange("p (a b) -> p a b", a=2), ACT.Sigmoid).then_inc(gates_ready, 1)
            for kv in range(2):
                for j in range(4):
                    split_high(act, B_CMP + 4 * kv + j + 2)
                act.wait_ge(tiles_used, B_CMP + 4 * (kv + 1))
                for c in range(2):
                    act.activation(cmp_hid[:, kv, c, :], psum[:, 2 * kv + c, 0:2 * N_CMP],
                                   ACT.Gelu_apprx_tanh).then_inc(cmp_hid_ready, 1)

            for n in range(6):
                act.wait_ge(bias_turned, n + 1)
                act.activation(bias_t.rearrange("p h k -> p (h k)")[:, n * 512:(n + 1) * 512], psum[:, BIAS_BANKS[n], :],
                               ACT.Copy).then_inc(bias_ready, 1)

            batches = [0]
            for gi in range(4):
                qt, g = gi // 2, gi % 2
                nk = P * (qt + 1)
                for b in range(2):
                    act.wait_ge(logits_ready, 3 * gi + b + 1)
                    act.activation(zbuf[:, b, :, 0:nk], zbuf[:, b, :, 0:nk], ACT.Exp).then_inc(exps_ready, 1)
                act.wait_ge(logits_ready, 3 * gi + 3)
                act.activation(zbuf_c, zbuf_c, ACT.Exp).then_inc(exps_ready, 1)
                if gi >= 2:
                    act.wait_ge(heads_sum, gi - 1)
                for n in range(2 * (qt + 1) + 1):
                    rows = N_CMP if n == 2 * (qt + 1) else P
                    act.wait_ge(turned, batches[0] + 1)
                    act.activation(probs_t[0:rows, gi % 2, n, :], psum[0:rows, 5 + batches[0] % 2, :],
                                   ACT.Copy).then_inc(turned_copied, 1)
                    batches[0] += 1
                act.wait_ge(heads_sum, gi + 1)
                half = slice(g * HD, (g + 1) * HD)
                act.activation(mix[half, 0:REP, qt * P:(qt + 1) * P],
                               psum[half, 7, :].rearrange("p (a b) -> p a b", a=REP), ACT.Copy).then_inc(heads_ready, 1)

            act.wait_ge(heads_ready, 4)
            act.wait_ge(conv_ready, 1)
            high_x(X_MIX, lambda q: mix[:, 2 * q:2 * q + 2, :])
            for m in range(KD):
                split_high(act, B_OUT1 + m + 2)
                act.wait_ge(tiles_used, B_OUT1 + m + 1)
                act.activation(y1[:, m, :], psum[:, m % 4, 0:TX], ACT.Copy).then_inc(out1_ready, 1)
            norm_act(1, y1, TX, lambda: act.wait_ge(out1_ready, KD))
            norm_root_act(1, TX)
            norm_act(2, hx1, TX, lambda: act.wait_ge(norm_out, 1))
            norm_root_act(2, TX)
            high_norm(X_NORM2, 1, TX)

            def ffn_act(j, i=None):
                def trips(per, v):
                    return v if i is None else i * per + v

                par = j % 2
                act.wait_ge(ffn_taps, trips(2, j + 1))
                for half in range(2):
                    split_high(act, B_FFN + (3 * j + 1 if j else 2) + half, i)
                    act.wait_ge(tiles_used, trips(BODY, B_FFN + (3 * j + half if j else half + 1)))
                    act.activation(ffn_c[:, par, half, :], psum[:, 2 * par + half, 0:TX], ACT.Copy,
                                   scale=taps[:, par, 3 * half + 2:3 * half + 3]).then_inc(ffn_scaled, 1)
                act.wait_ge(ffn_conv_g, trips(2, j + 3))
                act.activation(ffn_g[:, par, :], ffn_c[:, par, 0, :], ACT.Gelu_apprx_tanh).then_inc(ffn_gelu, 1)
                if j > 0:
                    split_high(act, B_FFN + 3 * j + 3, i)
                act.wait_ge(ffn_whole, trips(2, j + 1))
                act.activation(h_hi[:, par, :], ffn_h[:, par, :], ACT.Copy).then_inc(hidden_high, 1)

            ffn_act(0)
            with act.Fori(0, (NF - 2) // 2) as i:
                ffn_act(1, i)
                ffn_act(2, i)
            ffn_act(NF - 1)
            split_high(act, B_FFN + 3 * NF + 1)
            act.wait_ge(tiles_used, B_FFN + 3 * NF)
            for m in range(4):
                act.activation(y1[:, 2 * m:2 * m + 2, :], psum[:, 4 + m, :].rearrange("p (a b) -> p a b", a=2),
                               ACT.Copy).then_inc(ffn_copied, 1)
            norm_act(3, y1, TX, lambda: act.wait_ge(ffn_copied, 4))
            norm_root_act(3, TX)

            norm_act(4, hx[:, :, :], T2, lambda: (act.wait_ge(meta_loaded, 16), act.wait_ge(norm_out, 2)))
            norm_root_act(4, T2)
            high_norm(X_NORM4, 2, T2)
            act.wait_ge(pads_zeroed, 2)
            act.sem_inc(in2_copied, BODY)

            def in2(k, i=None):
                split_high(act, B_IN2 + k + 2, i)
                act.wait_ge(tiles_used, trip(B_IN2 + k + 1, i))
                act.activation(z2[:, trip(k, i), 1:T2 + 1], psum[:, k % BODY, 0:T2], ACT.Copy).then_inc(in2_copied, 1)

            with act.Fori(0, 2) as i:
                for k in range(BODY):
                    in2(k, i)
            act.wait_ge(in2_copied, BODY + 12)
            act.activation(z2[:, 4:8, 1:T2 + 1], z2[:, 4:8, 1:T2 + 1], ACT.Sigmoid).then_inc(glu_sig, 1)
            for k in range(12, 22):
                in2(k)

            act.wait_ge(cv_diff, 1)
            act.activation(sq4, conv_y, ACT.Square).then_inc(cv_squares, 1)
            act.wait_ge(cv_mean, 2)
            act.activation(rms[:], rms[:], ACT.Sqrt).then_inc(cv_root, 1)
            act.wait_ge(cv_scaled, 1)
            for m in range(4):
                act.activation(conv_y[:, m, :], conv_y[:, m, :], ACT.Silu, scale=colv("ln_g", m, m + 1),
                               bias=colv("ln_b", m, m + 1)).then_inc(cv_out, 1)

            act.wait_ge(shifted, 1)
            act.activation(z2[0:HD, 20, 1:T2 + 1], z2[0:HD, 20, 1:T2 + 1], ACT.Tanh).then_inc(lowrank_ready, 1)
            act.activation(z2[:, 21, 1:T2 + 1], z2[:, 21, 1:T2 + 1], ACT.Sigmoid).then_inc(lowrank_ready, 1)
            for n, (dst, b) in enumerate(((logdec, "w0"), (a_gate, "a0"))):
                for m in range(4):
                    act.wait_ge(up_sum, 4 * n + m + 1)
                    act.activation(dst[:, m, :], psum[:, 4 * n + m, 0:T2], ACT.Sigmoid,
                                   bias=colv(b, m, m + 1)).then_inc(up_ready, 1)
            act.wait_ge(kk_raw, 1)
            act.activation(sq4, kk, ACT.Square).then_inc(kk_squares, 1)
            for m in range(4):
                act.wait_ge(up_sum, 9 + m)
                act.activation(gmul[:, m, :], psum[:, m, 0:T2], ACT.Copy).then_inc(up_ready, 1)
            act.wait_ge(kk_mean, 1)
            act.activation(k_new, k_new, ACT.Sqrt).then_inc(kk_root, 1)
            act.wait_ge(cums_ready, 1)
            act.activation(e_cum, cum, ACT.Exp).then_inc(cexp_ready, 1)
            act.activation(e_neg, cum, ACT.Exp, scale=-1.0).then_inc(cexp_ready, 1)
            act.activation(e_prev, e_prev, ACT.Exp).then_inc(cexp_ready, 1)
            act.activation(e_end, e_end, ACT.Exp).then_inc(cexp_ready, 1)
            act.activation(chunk_decay, cum[:, :, CH - 1:T2:CH], ACT.Exp).then_inc(cexp_ready, 1)

            for tg in range(3):
                nt = min(P, T2 - tg * P)
                for n in range(4):
                    act.wait_ge(tm_sum, 4 * tg + n + 1)
                    act.activation(tm[0:nt, n, :], psum[0:nt, n, :], ACT.Copy).then_inc(tm_ready, 1)
                for hh in range(2):
                    u = 2 * tg + hh

                    def power(k, bank, dst):
                        act.wait_ge(pow_sum, 5 * u + k)
                        act.activation(gram[0:nt, dst, :, 0:nt], by_head(psum[0:nt, bank, :])[:, :, 0:nt],
                                       ACT.Copy).then_inc(pow_ready, 1)

                    act.wait_ge(mv_sum, u + 1)
                    act.activation(ycol[0:nt, :, 0:HD], tm[0:nt, 0, 4 * hh * HD:4 * (hh + 1) * HD].rearrange("p (h k) -> p h k", h=4),
                                   ACT.Copy).then_inc(y_ready, 1)
                    act.activation(ycol[0:nt, :, HD:P], by_head(psum[0:nt, 1, :])[:, :, 0:HD], ACT.Copy).then_inc(y_ready, 1)
                    power(1, 6, G_L2)
                    power(2, 7, G_L2T)
                    power(3, 2, G_L4)
                    power(4, 3, G_L4T)
                    power(5, 6, G_L8T)
                    if tg < 2:
                        for p in range(2):
                            act.wait_ge(fg_sum, 2 * u + p + 1)
                            act.activation(g_c[:, 2 * hh + p].rearrange("p a b -> p (a b)"), psum[:, 7, :],
                                           ACT.Copy).then_inc(g_ready, 1)

            split_high(act, B_MID + 2)
            act.wait_ge(gn_mean, 1)
            act.activation(gn_s, gn_s, ACT.Sqrt).then_inc(gn_root, 1)
            for g in range(16):
                if g > 0:
                    split_high(act, B_MID + g + 2)
                act.wait_ge(tiles_used, B_MID + g + 1)
                act.activation(gate_z[:, g, :], psum[:, g % 4, 0:TX], ACT.Sigmoid).then_inc(gate_sig, 1)
            act.wait_ge(cv_out, 4)
            act.wait_ge(mid_ready, 1)
            high_x(X_BRANCH, branch_in)
            for m in range(KD):
                split_high(act, B_MID + 16 + m + 2)
            act.wait_ge(tiles_used, B_MID + 3 * KD)
            high_x(X_MERGED, lambda q: merged[:, 2 * q:2 * q + 2, :], lambda q: act.wait_ge(merged_ready, 2 * q + 2))
            for m in range(KD):
                split_high(act, B_OUT2 + m + 2)
            norm_act(5, hx1, TX, lambda: act.wait_ge(out2_added, KD))
            norm_root_act(5, TX)
            high_norm(X_NORM5, 3, TX)

            for m in range(16):
                split_high(act, B_Q + m + 2)
                act.wait_ge(tiles_used, B_Q + m + 1)
                act.activation(query[:, m, :], psum[:, m % 4, 0:TX], ACT.Copy).then_inc(q_copied, 1)
            for n in range(2):
                split_high(act, B_SUB + n + 2)
                for qt in range(2):
                    for b in range(2):
                        if qt + b == 2:
                            act.wait_ge(tiles_used, B_SUB + n + 1)
                        else:
                            act.wait_ge(score_sum, 3 * n + 2 * qt + b + 1)
                        act.activation(score[:, qt, 8 * n + 4 * b:8 * n + 4 * b + 4, :].rearrange("p a b -> p (a b)"),
                                       psum[:, 4 * qt + b, :], ACT.Copy).then_inc(score_copied, 1)

            act.sem_inc(expert_act, BODY)

            def expert(e, i=None):
                split_high(act, B_EXP + e + 2, i)
                act.wait_ge(tiles_used, trip(B_EXP + e + 1, i))
                act.activation(act_all[:, trip(e, i), :], psum[:, e % BODY, 0:TX], ACT.Gelu).then_inc(expert_act, 1)

            def experts_from(e0, e1):
                trips = (e1 - e0) // BODY
                if trips > 1:
                    with act.Fori(0, trips) as i:
                        for k in range(BODY):
                            expert(e0 + k, i)
                for e in range(e0 + trips * BODY if trips > 1 else e0, e1):
                    expert(e)

            done = 0
            for qt in range(2):
                experts_from(done, exp_turn[qt])
                done = exp_turn[qt]
                act.wait_ge(pick_shift, qt + 1)
                act.activation(pick_s, pick_s, ACT.Exp).then_inc(pick_exp, 1)
            experts_from(done, FREE_EXPERTS)
            act.wait_ge(chosen_ready, 2)
            experts_from(FREE_EXPERTS, NE)

            act.wait_ge(chosen_turned, 4)
            with act.Fori(0, TX // 8) as i:
                for s in range(2):
                    act.wait_ge(gates_used, i * 2 + (s + 1))
                    for t in range(3):
                        ins = act.activation(off_1[:, s, t, :], const("iota"), ACT.Abs, scale=-1.0,
                                             bias=chosen_t[:, 2, bass.ds(i * 8 + (4 * s + t), 1)])
                    ins.then_inc(off_ready, 1)
                    act.wait_ge(off_ready, i * 2 + (s + 1))
                    for t in range(3):
                        ins = act.activation(hot_1[:, s, t, :], off_1[:, s, t, :].bitcast(F32), ACT.Relu,
                                             scale=chosen_t[:, 1, bass.ds(i * 8 + (4 * s + t), 1)],
                                             bias=chosen_t[:, 0, bass.ds(i * 8 + (4 * s + t), 1)])
                    ins.then_inc(hot_a, 1)

            def high_coef(e, i=None, first=False):
                if not first:
                    act.wait_ge(tiles_used, trip(B_V + e - 1, i))
                act.activation(h_hi[:, e % 2, :], act_all[:, trip(e, i), :], ACT.Copy).then_inc(coef_high, 1)

            act.wait_ge(gates_used, 2 + TX // 4)
            high_coef(0, first=True)
            high_coef(1, first=True)
            split_high(act, B_V + 2)

            def second(k, i=None):
                high_coef(k + 2, i)
                split_high(act, B_V + k + 3, i)

            pieces(B_V, NE - 3, act, second)
            high_coef(NE - 1)
            norm_act(6, hx1, TX, lambda: act.wait_ge(out3_added, 4))
            norm_root_act(6, TX)


def kernel(**inputs):
    import numpy as np
    import concourse.bacc as bacc
    from concourse.bass_utils import run_bass_kernel_spmd

    a = {name: np.asarray(value) for name, value in inputs.items()}
    depth1 = {name: (v[0] if v.ndim > 1 and v.shape[0] == 1 else v) for name, v in a.items()}
    g = depth1

    def vec(v):
        return v.reshape(-1, P).T

    def taps(v):
        t, n = v.shape
        return v.reshape(t, n // P, P).transpose(2, 1, 0).reshape(P, -1)

    def tiles(w):
        k, n = w.shape
        return w.reshape(k // P, P, n // P, P).transpose(2, 1, 0, 3).reshape(n // P, P, -1)

    w = g["w_in"]
    heads = [w[:, h * HD:(h + 1) * HD] for i in range(REP) for h in (i, i + REP)]
    kv0 = N_HEADS * HD
    at = lambda n: w[:, kv0 + n * HD:kv0 + (n + 1) * HD]
    pairs = [at(n) for n in (0, 0, 1, 1, 2, 2, 3, 3)]
    gate0 = kv0 + 12 * HD
    w1_in = tiles(np.concatenate(heads + pairs + [w[:, kv0 + 4 * HD:gate0], w[:, gate0 + 24:]], 1))
    wg = w[:, gate0:gate0 + 24].reshape(KD, P, N_HEADS, 3).transpose(1, 0, 3, 2).reshape(P, KD * 24)

    def cmp_tiles(w1):
        return w1.reshape(2, 4, 4, HD, 2 * P).transpose(1, 0, 3, 2, 4).reshape(4, P, TW)

    w1_cmp = np.concatenate([cmp_tiles(g["w_cmp_k1"]), cmp_tiles(g["w_cmp_v1"])], 0)
    w_out = g["w_out"]
    order = [w_out[h * HD:(h + 1) * HD] for i in range(REP) for h in (i, i + REP)]
    w1_out = tiles(np.concatenate(order + [w_out[N_HEADS * HD:]], 0))
    up = tiles(g["w_ffn_up"]).reshape(2, NF, P, TW)
    dn = g["w_ffn_down"].reshape(NF, P, TW)
    w1_ffn = np.stack([t for j in range(NF + 1) for t in ([up[0, j], up[1, j]] if j < NF else [])
                       + ([dn[j - 1]] if j else [])], 0)
    fc = g["ffn_conv_w"].reshape(3, 2, NF, P).transpose(3, 2, 1, 0).reshape(P, -1)
    pe = np.concatenate([g[n].reshape(2, 16, HD).transpose(0, 2, 1).reshape(P, 16) for n in ("pe_cmp_k", "pe_cmp_v")], 1)
    w2k = g["w_cmp_k2"].reshape(2, P, HD)
    w2k = np.concatenate([w2k, w2k], 2).transpose(1, 0, 2).reshape(P, 2 * P)
    w2v = g["w_cmp_v2"].reshape(2, P, HD).transpose(1, 0, 2).reshape(P, P)

    columns = {
        "mix_pre": vec(g["norm_mix_pre"]), "mix_post": vec(g["norm_mix_post"]), "ffn_pre": vec(g["norm_ffn_pre"]),
        "ffn_post": vec(g["norm_ffn_post"]), "mix2": vec(g["g_mix_2"]), "ffn2": vec(g["g_ffn_2"]),
        "final": vec(g["g_final_2"]), "conv_mix": taps(g["conv_mix_w"]), "ffn_conv": fc, "pe": pe, "gates": wg,
        "w2k": w2k, "w2v": w2v, "conv_w": taps(g["conv_w_2"]), "conv_b": vec(g["conv_b_2"]),
        "ln_g": vec(g["conv_ln_g_2"]), "ln_b": vec(g["conv_ln_b_2"]), "mu": vec(g["mu_shift_2"]), "w0": vec(g["w0_2"]),
        "a0": vec(g["a0_2"]), "k_k": vec(g["k_k_2"]), "k_a": vec(g["k_a_2"]), "r_k": vec(g["r_k_2"].reshape(-1)),
        "gn_g": vec(g["gn_g_2"]), "gn_b": vec(g["gn_b_2"]),
        "wa_up": np.concatenate([g["w_up_2"], g["a_up_2"]], 0), "g_up": g["g_up_2"],
    }
    columns.update(shape_constants())
    kept, first, second = (np.concatenate([columns[name] for name in part], 1) for part in (KEPT, FIRST, SECOND))

    w2 = tiles(g["w_in_2"])
    w2_in = w2[:22]
    branches = tiles(np.concatenate([g["w_conv_out_2"], g["w_rwkv_out_2"]], 0))
    w2_mid = np.concatenate([w2[22:38], branches], 0)
    w2_out = tiles(g["w_o_2"])
    w2_q = tiles(g["w_q_2"])
    w2_sub = g["sub_keys_2"].reshape(2, 8, NE, P).transpose(0, 3, 1, 2).reshape(2, P, TW)
    eu = g["expert_u_2"].reshape(NE, NE, KD, P)
    ev = g["expert_v_2"].reshape(NE, NE, TW)
    experts = np.concatenate([eu.transpose(1, 3, 2, 0).reshape(NE, P, TW), ev.transpose(1, 0, 2)], 0)

    arrays = {
        "x_t": a["x"].reshape(TX, KD, P).transpose(2, 1, 0), "meta_t": g["meta_tokens_2"].reshape(N_META, KD, P).transpose(2, 1, 0),
        "kept": kept, "first": first, "second": second, "rel": a["rel_bias"].T, "w1_in": w1_in, "w1_cmp": w1_cmp,
        "w1_out": w1_out, "w1_ffn": w1_ffn, "w2_in": w2_in, "w2_mid": w2_mid, "w2_out": w2_out, "w2_q": w2_q,
        "w2_sub": w2_sub, "experts": experts,
    }
    arrays = {name: np.ascontiguousarray(v) for name, v in arrays.items()}
    nc = bacc.Bacc("TRN2", target_bir_lowering=False, num_devices=1)
    ins = [nc.dram_tensor(name, v.shape, F32, kind="ExternalInput").ap() for name, v in arrays.items()]
    out = nc.dram_tensor("out_t", (P, KD, TX), F32, kind="ExternalOutput").ap()
    rows = nc.dram_tensor("bias_rows", (N_HEADS, 512), F32, kind="Internal").ap()
    bass_transformer_pair(nc, *ins, out, rows)
    got = run_bass_kernel_spmd(nc, [arrays], core_ids=[0]).results[0]["out_t"]
    return got.transpose(2, 1, 0).reshape(1, TX, D)
```
